# Optimizing a Trainium2 kernel written in Bass

```python
import math
import jax
import jax.numpy as jnp
from jax import lax
import numpy as np

D_MODEL = 1024
BATCH = 1
SEQ = 256
DEPTH = 2

GDN_HEADS = 4
GDN_DK = 128
GDN_DV = 128
CONV_WIDTH = 4
GDN_CHUNK = 64
ATT_HEADS = 4
ATT_DH = 128
IDX_HEADS = 4
IDX_DH = 64
TOPK_MAX = 256
Q_BLOCK = 128
GLA_HEADS = 4
GLA_DK = D_MODEL // 2 // GLA_HEADS
GLA_DV = D_MODEL // GLA_HEADS
GLA_RANK = 16
GLA_TAU = 16.0
GLA_CHUNK = 64
N_GROUPS = 4
EXPERTS_PER_GROUP = 8
N_EXPERTS = N_GROUPS * EXPERTS_PER_GROUP
TOP_K_EXPERTS = 2
D_EXPERT = 512
MOE_BLOCK = 128
ROPE_THETA = 10000.0
EPS = 1e-6

GDN_QK = GDN_HEADS * GDN_DK
GDN_V = GDN_HEADS * GDN_DV
ATT_W = ATT_HEADS * ATT_DH
EVEN_SPLITS = [GDN_QK, GDN_QK, GDN_V, GDN_V, GDN_HEADS, GDN_HEADS,
               ATT_W, ATT_W, ATT_W, IDX_HEADS * IDX_DH, IDX_DH, IDX_HEADS]
EVEN_IN = int(sum(EVEN_SPLITS))
EVEN_MIX = GDN_V + ATT_W
ODD_SPLITS = [GLA_HEADS * GLA_DK, GLA_HEADS * GLA_DK, GLA_HEADS * GLA_DV,
              GLA_HEADS * GLA_DV, GLA_RANK]
ODD_IN = int(sum(ODD_SPLITS))
ODD_MIX = GLA_HEADS * GLA_DV


F32 = jnp.float32

def split_cols(t, sizes):
    idx = np.cumsum(sizes)[:-1].tolist()
    return jnp.split(t, idx, axis=-1)

def rms_norm(t, g):
    tf = t.astype(F32)
    y = tf * lax.rsqrt(jnp.mean(tf * tf, axis=-1, keepdims=True) + EPS)
    return (y * g.astype(F32)).astype(t.dtype)

def l2_normalize(t):
    tf = t.astype(F32)
    return (tf * lax.rsqrt(jnp.sum(tf * tf, axis=-1, keepdims=True) + EPS)).astype(t.dtype)

def modulate(hn, shift, scale):
    return hn * (1 + scale[:, None, :]) + shift[:, None, :]

def rope_tables(positions, dim):
    inv = 1.0 / (ROPE_THETA ** (jnp.arange(0, dim, 2, dtype=F32) / dim))
    ang = positions.astype(F32)[..., None] * inv
    return jnp.cos(ang), jnp.sin(ang)

def apply_rope(t, cos, sin):
    t1, t2 = jnp.split(t.astype(F32), 2, axis=-1)
    c = cos[:, :, None, :]
    s = sin[:, :, None, :]
    return jnp.concatenate([t1 * c - t2 * s, t2 * c + t1 * s], axis=-1).astype(t.dtype)

def causal_depthwise_conv(t, w):
    width = w.shape[0]
    return lax.conv_general_dilated(
        t, w[:, None, :].astype(t.dtype), window_strides=(1,),
        padding=((width - 1, 0),), dimension_numbers=('NWC', 'WIO', 'NWC'),
        feature_group_count=t.shape[-1])

def to_chunks(t, chunk):
    b, s, h = t.shape[:3]
    t = t.reshape((b, s // chunk, chunk, h) + t.shape[3:])
    return t.transpose((1, 0, 3, 2) + tuple(range(4, t.ndim)))

def from_chunks(t):
    n, b, h, c = t.shape[:4]
    t = t.transpose((1, 0, 3, 2) + tuple(range(4, t.ndim)))
    return t.reshape((b, n * c, h) + t.shape[4:])

def gated_delta_rule(q, k, v, g, beta):
    dtype = v.dtype
    b_, _, h, dk = q.shape
    dv = v.shape[-1]
    c = GDN_CHUNK
    q = to_chunks(q.astype(F32) * dk ** -0.5, c)
    k = to_chunks(k.astype(F32), c)
    v = to_chunks(v.astype(F32), c)
    g = to_chunks(g.astype(F32), c)
    beta = to_chunks(beta.astype(F32), c)
    gc = jnp.cumsum(g, axis=-1)
    incl = jnp.tril(jnp.ones((c, c), bool))
    strict = jnp.tril(jnp.ones((c, c), bool), -1)
    decay = jnp.exp(jnp.where(incl, gc[..., :, None] - gc[..., None, :], -jnp.inf))
    kb = k * beta[..., None]
    lmat = jnp.where(strict, jnp.einsum('nbhid,nbhjd->nbhij', kb, k) * decay, 0.0)
    eye = jnp.eye(c, dtype=F32)
    tmat = lax.linalg.triangular_solve(eye + lmat, jnp.broadcast_to(eye, lmat.shape),
                                       left_side=True, lower=True, unit_diagonal=True)
    w = tmat @ (kb * jnp.exp(gc)[..., None])
    u = tmat @ (v * beta[..., None])
    aqk = jnp.einsum('nbhid,nbhjd->nbhij', q, k) * decay
    qg = q * jnp.exp(gc)[..., None]
    glast = gc[..., -1:]
    kd = k * jnp.exp(glast - gc)[..., None]

    def step(state, xs):
        qg_i, aqk_i, w_i, u_i, kd_i, gl_i = xs
        v_new = u_i - w_i @ state
        o = qg_i @ state + aqk_i @ v_new
        state = state * jnp.exp(gl_i)[..., None] + jnp.swapaxes(kd_i, -1, -2) @ v_new
        return state, o

    s0 = jnp.zeros((b_, h, dk, dv), F32)
    _, o = lax.scan(step, s0, (qg, aqk, w, u, kd, glast))
    return from_chunks(o).astype(dtype)

def gla_chunked(q, k, v, log_a):
    dtype = v.dtype
    b_, _, h, dk = q.shape
    dv = v.shape[-1]
    c = GLA_CHUNK
    q = to_chunks(q.astype(F32) * dk ** -0.5, c)
    k = to_chunks(k.astype(F32), c)
    v = to_chunks(v.astype(F32), c)
    bcum = jnp.cumsum(to_chunks(log_a.astype(F32), c), axis=-2)
    incl = jnp.tril(jnp.ones((c, c), bool))

    def step(state, xs):
        q_i, k_i, v_i, b_i = xs
        bl = b_i[..., -1:, :]
        o_inter = (q_i * jnp.exp(b_i)) @ state
        diff = jnp.where(incl[..., None], b_i[..., :, None, :] - b_i[..., None, :, :], -jnp.inf)
        att = jnp.einsum('bhid,bhjd,bhijd->bhij', q_i, k_i, jnp.exp(diff))
        o = o_inter + att @ v_i
        state = (state * jnp.swapaxes(jnp.exp(bl), -1, -2)
                 + jnp.swapaxes(k_i * jnp.exp(bl - b_i), -1, -2) @ v_i)
        return state, o

    s0 = jnp.zeros((b_, h, dk, dv), F32)
    _, o = lax.scan(step, s0, (q, k, v, bcum))
    return from_chunks(o).astype(dtype)

def dsa_sparse_attention(q, k, v, q_idx, k_idx, w_idx):
    b_, s_, h, dh = q.shape
    topk = min(TOPK_MAX, s_ // 4)
    nblk = s_ // Q_BLOCK
    key_pos = jnp.arange(s_)
    k_idx32 = k_idx.astype(F32)

    def blockify(t):
        return jnp.swapaxes(t.reshape((b_, nblk, Q_BLOCK) + t.shape[2:]), 0, 1)

    def one_block(args):
        q_b, qi_b, wi_b, start = args
        q_pos = start + jnp.arange(Q_BLOCK)
        dots = jnp.einsum('bqhd,bsd->bqhs', qi_b.astype(F32), k_idx32)
        score = jnp.einsum('bqh,bqhs->bqs', wi_b.astype(F32), jax.nn.relu(dots))
        causal = key_pos[None, :] <= q_pos[:, None]
        score = jnp.where(causal[None], score, -jnp.inf)
        _, sel = lax.top_k(score, topk)
        k_sel = jax.vmap(lambda kk, ii: kk[ii])(k, sel)
        v_sel = jax.vmap(lambda vv, ii: vv[ii])(v, sel)
        logits = jnp.einsum('bqhd,bqkhd->bqhk', q_b, k_sel).astype(F32) * dh ** -0.5
        valid = sel <= q_pos[None, :, None]
        logits = jnp.where(valid[:, :, None, :], logits, -jnp.inf)
        p = jax.nn.softmax(logits, axis=-1).astype(v.dtype)
        return jnp.einsum('bqhk,bqkhd->bqhd', p, v_sel)

    starts = jnp.arange(nblk) * Q_BLOCK
    out = lax.map(one_block, (blockify(q), blockify(q_idx), blockify(w_idx), starts))
    return jnp.swapaxes(out, 0, 1).reshape(b_, s_, h, dh)

def even_mixer(h, cos_a, sin_a, cos_i, sin_i, w_in, conv_w, a_log, dt_bias, out_norm, w_out):
    b_, s_, _ = h.shape
    heads = lambda t, n: t.reshape(b_, s_, n, -1)
    proj = h @ w_in
    qa, ka, va, za, ba, aa, qb, kb, vb, qi, ki, wi = split_cols(proj, EVEN_SPLITS)
    qkv = jax.nn.silu(causal_depthwise_conv(jnp.concatenate([qa, ka, va], axis=-1), conv_w))
    qa, ka, va = split_cols(qkv, [GDN_QK, GDN_QK, GDN_V])
    qa = l2_normalize(heads(qa, GDN_HEADS))
    ka = l2_normalize(heads(ka, GDN_HEADS))
    va = heads(va, GDN_HEADS)
    beta = jax.nn.sigmoid(ba.astype(F32))
    g = -jnp.exp(a_log.astype(F32)) * jax.nn.softplus(aa.astype(F32) + dt_bias.astype(F32))
    oa = gated_delta_rule(qa, ka, va, g, beta)
    oa = rms_norm(oa, out_norm) * jax.nn.silu(heads(za, GDN_HEADS))
    qb = apply_rope(heads(qb, ATT_HEADS), cos_a, sin_a)
    kb = apply_rope(heads(kb, ATT_HEADS), cos_a, sin_a)
    vb = heads(vb, ATT_HEADS)
    qi = apply_rope(heads(qi, IDX_HEADS), cos_i, sin_i)
    ki = apply_rope(ki[:, :, None, :], cos_i, sin_i)[:, :, 0, :]
    wi = wi * (IDX_HEADS * IDX_DH) ** -0.5
    ob = dsa_sparse_attention(qb, kb, vb, qi, ki, wi)
    o = jnp.concatenate([oa.reshape(b_, s_, -1), ob.reshape(b_, s_, -1)], axis=-1)
    return o @ w_out

def gla_mixer(h, w_in, w_gate2, b_gate2, out_norm, w_out):
    b_, s_, _ = h.shape
    heads = lambda t: t.reshape(b_, s_, GLA_HEADS, -1)
    proj = h @ w_in
    q, k, v, r, glr = split_cols(proj, ODD_SPLITS)
    log_a = jax.nn.log_sigmoid((glr @ w_gate2 + b_gate2).astype(F32)) / GLA_TAU
    o = gla_chunked(heads(q), heads(k), heads(v), heads(log_a))
    o = rms_norm(o, out_norm) * jax.nn.silu(heads(r))
    return o.reshape(b_, s_, -1) @ w_out

def hier_moe(h, wg, bg, we, be, w1, w3, w2):
    b_, s_, d = h.shape
    t = b_ * s_
    xt = h.reshape(t, d)
    tok_ids = jnp.arange(t)
    g_logits = (xt @ wg + bg).astype(F32)
    g_prob = jax.nn.softmax(g_logits, axis=-1)
    g_sel = jnp.argmax(g_logits, axis=-1)
    g_gate = g_prob[tok_ids, g_sel]
    e_logits = (jnp.einsum('td,gde->tge', xt, we) + be).astype(F32)
    e_logits = e_logits[tok_ids, g_sel]
    top_l, top_i = lax.top_k(e_logits, TOP_K_EXPERTS)
    gates = g_gate[:, None] * jax.nn.softmax(top_l, axis=-1)
    eid = (g_sel[:, None] * EXPERTS_PER_GROUP + top_i).reshape(-1).astype(jnp.int32)
    wts = gates.reshape(-1)
    tok = jnp.repeat(tok_ids.astype(jnp.int32), TOP_K_EXPERTS)
    m = t * TOP_K_EXPERTS
    counts = jnp.bincount(eid, length=N_EXPERTS)
    padded = ((counts + MOE_BLOCK - 1) // MOE_BLOCK) * MOE_BLOCK
    pad_end = jnp.cumsum(padded)
    pad_start = pad_end - padded
    raw_start = jnp.cumsum(counts) - counts
    order = jnp.argsort(eid)
    se = eid[order]
    dest = pad_start[se] + (jnp.arange(m) - raw_start[se])
    p_rows = (-(-m // MOE_BLOCK) + N_EXPERTS) * MOE_BLOCK
    buf_tok = jnp.zeros((p_rows,), jnp.int32).at[dest].set(tok[order])
    buf_w = jnp.zeros((p_rows,), F32).at[dest].set(wts[order])
    nblk = p_rows // MOE_BLOCK
    blk_exp = jnp.clip(jnp.searchsorted(pad_end, jnp.arange(nblk) * MOE_BLOCK, side='right'),
                       0, N_EXPERTS - 1)
    xb = xt[buf_tok].reshape(nblk, MOE_BLOCK, d)

    def expert_block(args):
        xi, e = args
        hid = jax.nn.silu(xi @ w1[e]) * (xi @ w3[e])
        return hid @ w2[e]

    yb = lax.map(expert_block, (xb, blk_exp)).reshape(p_rows, d)
    y = jnp.zeros((t, d), h.dtype).at[buf_tok].add(yb * buf_w[:, None].astype(yb.dtype))
    return y.reshape(b_, s_, d)

def first_inputs(seed: int = 0) -> dict:
    key = jax.random.key(seed)
    d = D_MODEL
    n_even = (DEPTH + 1) // 2
    n_odd = DEPTH // 2

    def nrm(i, shape, scale):
        return jax.random.normal(jax.random.fold_in(key, i), shape, F32) * scale

    def gain(i, shape):
        return 1.0 + nrm(i, shape, 0.02)

    return {
        "x": nrm(0, (BATCH, SEQ, d), 1.0),
        "c": nrm(1, (BATCH, d), 1.0),
        "positions": jnp.broadcast_to(jnp.arange(SEQ, dtype=jnp.int32), (BATCH, SEQ)),
        "ada_w": nrm(2, (DEPTH, d, 6 * d), 0.5 * d ** -0.5),
        "ada_b": nrm(3, (DEPTH, 6 * d), 0.02),
        "norm_mix": gain(4, (DEPTH, d)),
        "norm_ffn": gain(5, (DEPTH, d)),
        "even_w_in": nrm(6, (n_even, d, EVEN_IN), d ** -0.5),
        "gdn_conv_w": nrm(7, (n_even, CONV_WIDTH, 2 * GDN_QK + GDN_V), CONV_WIDTH ** -0.5),
        "gdn_a_log": jnp.log(jax.random.uniform(jax.random.fold_in(key, 8), (n_even, GDN_HEADS), F32, 1.0, 16.0)),
        "gdn_dt_bias": nrm(9, (n_even, GDN_HEADS), 0.1),
        "gdn_out_norm": gain(10, (n_even, GDN_DV)),
        "even_w_out": nrm(11, (n_even, EVEN_MIX, d), EVEN_MIX ** -0.5),
        "gla_w_in": nrm(12, (n_odd, d, ODD_IN), d ** -0.5),
        "gla_w_gate2": nrm(13, (n_odd, GLA_RANK, GLA_HEADS * GLA_DK), GLA_RANK ** -0.5),
        "gla_b_gate2": nrm(14, (n_odd, GLA_HEADS * GLA_DK), 0.1),
        "gla_out_norm": gain(15, (n_odd, GLA_DV)),
        "gla_w_out": nrm(16, (n_odd, ODD_MIX, d), ODD_MIX ** -0.5),
        "router_group_w": nrm(17, (DEPTH, d, N_GROUPS), d ** -0.5),
        "router_group_b": nrm(18, (DEPTH, N_GROUPS), 0.01),
        "router_exp_w": nrm(19, (DEPTH, N_GROUPS, d, EXPERTS_PER_GROUP), d ** -0.5),
        "router_exp_b": nrm(20, (DEPTH, N_GROUPS, EXPERTS_PER_GROUP), 0.01),
        "exp_w1": nrm(21, (DEPTH, N_EXPERTS, d, D_EXPERT), d ** -0.5),
        "exp_w3": nrm(22, (DEPTH, N_EXPERTS, d, D_EXPERT), d ** -0.5),
        "exp_w2": nrm(23, (DEPTH, N_EXPERTS, D_EXPERT, d), D_EXPERT ** -0.5),
        "final_norm": gain(24, (d,)),
    }

def first_block(x, c, positions, ada_w, ada_b, norm_mix, norm_ffn,
              even_w_in, gdn_conv_w, gdn_a_log, gdn_dt_bias, gdn_out_norm, even_w_out,
              gla_w_in, gla_w_gate2, gla_b_gate2, gla_out_norm, gla_w_out,
              router_group_w, router_group_b, router_exp_w, router_exp_b,
              exp_w1, exp_w3, exp_w2, final_norm):
    cos_a, sin_a = rope_tables(positions, ATT_DH)
    cos_i, sin_i = rope_tables(positions, IDX_DH)
    cond = jax.nn.silu(c)
    for layer in range(DEPTH):
        mod = cond @ ada_w[layer] + ada_b[layer]
        sh_m, sc_m, gt_m, sh_f, sc_f, gt_f = jnp.split(mod, 6, axis=-1)
        h = modulate(rms_norm(x, norm_mix[layer]), sh_m, sc_m)
        i = layer // 2
        if layer % 2 == 0:
            mix = even_mixer(h, cos_a, sin_a, cos_i, sin_i, even_w_in[i], gdn_conv_w[i],
                             gdn_a_log[i], gdn_dt_bias[i], gdn_out_norm[i], even_w_out[i])
        else:
            mix = gla_mixer(h, gla_w_in[i], gla_w_gate2[i], gla_b_gate2[i],
                            gla_out_norm[i], gla_w_out[i])
        x = x + gt_m[:, None, :] * mix
        h = modulate(rms_norm(x, norm_ffn[layer]), sh_f, sc_f)
        x = x + gt_f[:, None, :] * hier_moe(h, router_group_w[layer], router_group_b[layer],
                                           router_exp_w[layer], router_exp_b[layer],
                                           exp_w1[layer], exp_w3[layer], exp_w2[layer])
    return rms_norm(x, final_norm)


N_BRANCH = 4
BRANCH_WIDTH = 256
HEAD_DIM = 64
N_HEADS = BRANCH_WIDTH // HEAD_DIM
MLA_Q_RANK = 256
MLA_KV_RANK = 128
MLA_NOPE_DIM = 64
MLA_ROPE_DIM = 32
MLA_V_DIM = BRANCH_WIDTH // N_HEADS
ROPE_BASE = 10000.0
CONV_CH = BRANCH_WIDTH
CONV_WIDTH_2 = 31
FORGET_BIAS_INIT = 3.0
N_EXPERTS_2 = N_GROUPS * EXPERTS_PER_GROUP
TOP_K = 2
EXPERT_FF = 256
ROW_BLOCK = 128
NORM_EPS = 1e-5
IN_SPLITS = (MLA_Q_RANK, MLA_KV_RANK, MLA_ROPE_DIM, 3 * BRANCH_WIDTH, 2 * CONV_CH, 3 * BRANCH_WIDTH, N_HEADS, N_BRANCH * D_MODEL)
N_IN = sum(IN_SPLITS)


def _layernorm(x, g, b):
    xf = x.astype(jnp.float32)
    mu = jnp.mean(xf, axis=-1, keepdims=True)
    var = jnp.mean(jnp.square(xf - mu), axis=-1, keepdims=True)
    y = (xf - mu) * lax.rsqrt(var + NORM_EPS) * g.astype(jnp.float32) + b.astype(jnp.float32)
    return y.astype(x.dtype)

def _rmsnorm(x, g):
    xf = x.astype(jnp.float32)
    y = xf * lax.rsqrt(jnp.mean(xf * xf, axis=-1, keepdims=True) + NORM_EPS) * g.astype(jnp.float32)
    return y.astype(x.dtype)

def _rope(x, positions):
    half = x.shape[-1] // 2
    inv = ROPE_BASE ** (-jnp.arange(half, dtype=jnp.float32) / half)
    ang = (positions.astype(jnp.float32)[..., None] * inv)[:, :, None, :]
    cos, sin = jnp.cos(ang), jnp.sin(ang)
    x1 = x[..., :half].astype(jnp.float32)
    x2 = x[..., half:].astype(jnp.float32)
    out = jnp.concatenate([x1 * cos - x2 * sin, x2 * cos + x1 * sin], axis=-1)
    return out.astype(x.dtype)

def _split_cols(z):
    idx = [int(i) for i in np.cumsum(IN_SPLITS)[:-1]]
    return jnp.split(z, idx, axis=-1)

def _split_heads(qkv):
    b, s, _ = qkv.shape
    qkv = qkv.reshape(b, s, 3, N_HEADS, HEAD_DIM).transpose(2, 0, 3, 1, 4)
    return qkv[0], qkv[1], qkv[2]

def _merge_heads(o):
    b, h, s, d = o.shape
    return o.transpose(0, 2, 1, 3).reshape(b, s, h * d)

def _sweep_query_blocks(block_fn, q_side):
    b, h, s = q_side[0].shape[:3]
    nb = s // Q_BLOCK
    blocks = tuple(jnp.moveaxis(a.reshape((b, h, nb, Q_BLOCK) + a.shape[3:]), 2, 0) for a in q_side)
    t_pos = jnp.arange(s, dtype=jnp.int32).reshape(nb, Q_BLOCK)
    out = lax.map(lambda args: block_fn(*args), (t_pos,) + blocks)
    return jnp.moveaxis(out, 0, 2).reshape(b, h, s, out.shape[-1])

def _mla(c_q, c_kv, k_rope_raw, positions, q_norm, kv_norm, w_uq, w_ukv):
    b, s, _ = c_q.shape
    q = (_rmsnorm(c_q, q_norm) @ w_uq).reshape(b, s, N_HEADS, MLA_NOPE_DIM + MLA_ROPE_DIM)
    q_nope = q[..., :MLA_NOPE_DIM].transpose(0, 2, 1, 3)
    q_rope = _rope(q[..., MLA_NOPE_DIM:], positions).transpose(0, 2, 1, 3)
    kv = (_rmsnorm(c_kv, kv_norm) @ w_ukv).reshape(b, s, N_HEADS, MLA_NOPE_DIM + MLA_V_DIM)
    k_nope = kv[..., :MLA_NOPE_DIM].transpose(0, 2, 1, 3)
    v = kv[..., MLA_NOPE_DIM:].transpose(0, 2, 1, 3)
    k_rope = _rope(k_rope_raw[:, :, None, :], positions)[:, :, 0, :]
    scale = (MLA_NOPE_DIM + MLA_ROPE_DIM) ** -0.5
    key_pos = jnp.arange(s, dtype=jnp.int32)

    def block(t_pos, qn, qr):
        logits = jnp.einsum('bhqd,bhkd->bhqk', qn, k_nope) + jnp.einsum('bhqr,bkr->bhqk', qr, k_rope)
        logits = logits.astype(jnp.float32) * scale
        logits = jnp.where(key_pos[None, :] <= t_pos[:, None], logits, -jnp.inf)
        p = jax.nn.softmax(logits, axis=-1).astype(v.dtype)
        return jnp.einsum('bhqk,bhkd->bhqd', p, v)

    return _merge_heads(_sweep_query_blocks(block, (q_nope, q_rope)))

def _stick_breaking(q, k, v):
    s = k.shape[2]
    scale = HEAD_DIM ** -0.5
    key_pos = jnp.arange(s, dtype=jnp.int32)

    def block(t_pos, qb):
        z = jnp.einsum('bhqd,bhkd->bhqk', qb, k).astype(jnp.float32) * scale
        strict = key_pos[None, :] < t_pos[:, None]
        log_stay = jnp.where(strict, jax.nn.log_sigmoid(-z), 0.0)
        after = lax.cumsum(log_stay, axis=3, reverse=True) - log_stay
        a = jnp.where(strict, jnp.exp(jax.nn.log_sigmoid(z) + after), 0.0).astype(v.dtype)
        return jnp.einsum('bhqk,bhkd->bhqd', a, v)

    return _merge_heads(_sweep_query_blocks(block, (q,)))

def _conformer_conv(u, conv_w, conv_b, ln_g, ln_b):
    a, g = jnp.split(u, 2, axis=-1)
    h = a * jax.nn.sigmoid(g)
    hp = jnp.pad(h, ((0, 0), (CONV_WIDTH_2 - 1, 0), (0, 0)))
    y = lax.conv_general_dilated(hp, conv_w[:, None, :], window_strides=(1,), padding='VALID',
                                 dimension_numbers=('NWC', 'WIO', 'NWC'), feature_group_count=CONV_CH)
    y = _layernorm(y + conv_b, ln_g, ln_b)
    return jax.nn.silu(y)

def _forgetting_attention(q, k, v, forget_logit, b_forget):
    s = k.shape[2]
    scale = HEAD_DIM ** -0.5
    log_f = jax.nn.log_sigmoid((forget_logit + b_forget).astype(jnp.float32))
    c = jnp.cumsum(log_f, axis=1).transpose(0, 2, 1)
    key_pos = jnp.arange(s, dtype=jnp.int32)

    def block(t_pos, qb, cb):
        logits = jnp.einsum('bhqd,bhkd->bhqk', qb, k).astype(jnp.float32) * scale
        logits = logits + cb[..., None] - c[:, :, None, :]
        logits = jnp.where(key_pos[None, :] <= t_pos[:, None], logits, -jnp.inf)
        p = jax.nn.softmax(logits, axis=-1).astype(v.dtype)
        return jnp.einsum('bhqk,bhkd->bhqd', p, v)

    return _merge_heads(_sweep_query_blocks(block, (q, c)))

def _token_mixer(x, positions, w_in, b_gate, b_forget, mla_q_norm, mla_kv_norm, mla_w_uq, mla_w_ukv,
                 conv_w, conv_b, conv_ln_g, conv_ln_b, w_branch, w_o):
    b, s, d = x.shape
    z = x @ w_in
    c_q, c_kv, k_rope, sb_qkv, conv_in, fox_qkv, fox_f, gate_logits = _split_cols(z)
    y_a = _mla(c_q, c_kv, k_rope, positions, mla_q_norm, mla_kv_norm, mla_w_uq, mla_w_ukv)
    y_b = _stick_breaking(*_split_heads(sb_qkv))
    y_c = _conformer_conv(conv_in, conv_w, conv_b, conv_ln_g, conv_ln_b)
    y_d = _forgetting_attention(*_split_heads(fox_qkv), fox_f, b_forget)
    ys = jnp.stack([y_a, y_b, y_c, y_d], axis=2)
    gates = jax.nn.sigmoid(gate_logits + b_gate).reshape(b, s, N_BRANCH, d)
    proj = jnp.einsum('bsnc,ncd->bsnd', ys, w_branch)
    merged = jnp.sum(proj * gates, axis=2)
    return merged @ w_o

def _hier_moe(h, w_rg, b_rg, w_re, b_re, w_gate, w_up, w_down):
    b, s, d = h.shape
    xt = h.reshape(-1, d)
    n_tok = xt.shape[0]
    grp_prob = jax.nn.softmax((xt @ w_rg + b_rg).astype(jnp.float32), axis=-1)
    grp_p, grp_idx = lax.top_k(grp_prob, 1)
    exp_logits = (xt @ w_re + b_re).astype(jnp.float32).reshape(n_tok, N_GROUPS, EXPERTS_PER_GROUP)
    in_grp = jnp.take_along_axis(exp_logits, grp_idx[:, :, None], axis=1)[:, 0]
    top_p, top_i = lax.top_k(jax.nn.softmax(in_grp, axis=-1), TOP_K)
    weights = grp_p * top_p / jnp.sum(top_p, axis=-1, keepdims=True)
    expert_id = (grp_idx * EXPERTS_PER_GROUP + top_i).reshape(-1)
    n_assign = expert_id.shape[0]
    order = jnp.argsort(expert_id).astype(jnp.int32)
    sorted_e = expert_id[order]
    counts = jnp.bincount(expert_id, length=N_EXPERTS_2).astype(jnp.int32)
    padded = (counts + ROW_BLOCK - 1) // ROW_BLOCK * ROW_BLOCK
    pad_end = jnp.cumsum(padded)
    pad_start = pad_end - padded
    start = jnp.cumsum(counts) - counts
    slot = pad_start[sorted_e] + jnp.arange(n_assign, dtype=jnp.int32) - start[sorted_e]
    n_blocks = (n_assign + ROW_BLOCK - 1) // ROW_BLOCK + N_EXPERTS_2
    slot_token = jnp.full((n_blocks * ROW_BLOCK,), n_tok, dtype=jnp.int32).at[slot].set(order // TOP_K)
    block_start = jnp.arange(n_blocks, dtype=jnp.int32) * ROW_BLOCK
    block_expert = jnp.minimum(jnp.searchsorted(pad_end, block_start, side='right'), N_EXPERTS_2 - 1)
    x_pad = jnp.concatenate([xt, jnp.zeros((1, d), xt.dtype)], axis=0)
    xb = x_pad[slot_token].reshape(n_blocks, ROW_BLOCK, d)

    def expert_block(args):
        xe, e = args
        hid = jax.nn.silu(xe @ w_gate[e]) * (xe @ w_up[e])
        return hid @ w_down[e]

    yb = lax.map(expert_block, (xb, block_expert)).reshape(-1, d)
    y_assign = jnp.zeros((n_assign, d), yb.dtype).at[order].set(yb[slot])
    y = jnp.einsum('tkd,tk->td', y_assign.reshape(n_tok, TOP_K, d), weights.astype(yb.dtype))
    return y.reshape(b, s, d)

def second_inputs(seed: int = 0) -> dict:
    key = jax.random.key(seed)
    ks = jax.random.split(key, 28)
    L, D = DEPTH, D_MODEL
    beta = (8.0 * DEPTH) ** -0.25

    def nrm(k, shape, scale):
        return jax.random.normal(k, shape, jnp.float32) * scale

    def gain(k, shape):
        return 1.0 + 0.02 * jax.random.normal(k, shape, jnp.float32)

    offset = jax.random.randint(ks[1], (BATCH, 1), 0, 1024, dtype=jnp.int32)
    positions = offset + jnp.arange(SEQ, dtype=jnp.int32)[None, :]
    return {
        'x': nrm(ks[0], (BATCH, SEQ, D), 1.0),
        'positions': positions,
        'w_in': nrm(ks[2], (L, D, N_IN), D ** -0.5),
        'b_gate': nrm(ks[3], (L, N_BRANCH * D), 0.02),
        'b_forget': FORGET_BIAS_INIT + nrm(ks[4], (L, N_HEADS), 0.1),
        'mla_q_norm': gain(ks[5], (L, MLA_Q_RANK)),
        'mla_kv_norm': gain(ks[6], (L, MLA_KV_RANK)),
        'mla_w_uq': nrm(ks[7], (L, MLA_Q_RANK, N_HEADS * (MLA_NOPE_DIM + MLA_ROPE_DIM)), MLA_Q_RANK ** -0.5),
        'mla_w_ukv': nrm(ks[8], (L, MLA_KV_RANK, N_HEADS * (MLA_NOPE_DIM + MLA_V_DIM)), MLA_KV_RANK ** -0.5),
        'conv_w': nrm(ks[9], (L, CONV_WIDTH_2, CONV_CH), CONV_WIDTH_2 ** -0.5),
        'conv_b': nrm(ks[10], (L, CONV_CH), 0.02),
        'conv_ln_g': gain(ks[11], (L, CONV_CH)),
        'conv_ln_b': nrm(ks[12], (L, CONV_CH), 0.02),
        'w_branch': nrm(ks[13], (L, N_BRANCH, BRANCH_WIDTH, D), BRANCH_WIDTH ** -0.5),
        'w_o': nrm(ks[14], (L, D, D), beta * D ** -0.5),
        'ln1_g': gain(ks[15], (L, D)),
        'ln1_b': nrm(ks[16], (L, D), 0.02),
        'w_router_group': nrm(ks[17], (L, D, N_GROUPS), D ** -0.5),
        'b_router_group': nrm(ks[18], (L, N_GROUPS), 0.01),
        'w_router_expert': nrm(ks[19], (L, D, N_EXPERTS_2), D ** -0.5),
        'b_router_expert': nrm(ks[20], (L, N_EXPERTS_2), 0.01),
        'w_exp_gate': nrm(ks[21], (L, N_EXPERTS_2, D, EXPERT_FF), D ** -0.5),
        'w_exp_up': nrm(ks[22], (L, N_EXPERTS_2, D, EXPERT_FF), D ** -0.5),
        'w_exp_down': nrm(ks[23], (L, N_EXPERTS_2, EXPERT_FF, D), beta * EXPERT_FF ** -0.5),
        'ln2_g': gain(ks[24], (L, D)),
        'ln2_b': nrm(ks[25], (L, D), 0.02),
    }

def second_block(x, positions, w_in, b_gate, b_forget, mla_q_norm, mla_kv_norm, mla_w_uq, mla_w_ukv,
              conv_w, conv_b, conv_ln_g, conv_ln_b, w_branch, w_o, ln1_g, ln1_b,
              w_router_group, b_router_group, w_router_expert, b_router_expert,
              w_exp_gate, w_exp_up, w_exp_down, ln2_g, ln2_b):
    alpha = (2.0 * DEPTH) ** 0.25
    for l in range(DEPTH):
        mix = _token_mixer(x, positions, w_in[l], b_gate[l], b_forget[l], mla_q_norm[l], mla_kv_norm[l],
                           mla_w_uq[l], mla_w_ukv[l], conv_w[l], conv_b[l], conv_ln_g[l], conv_ln_b[l],
                           w_branch[l], w_o[l])
        x = _layernorm(alpha * x + mix, ln1_g[l], ln1_b[l])
        ffn = _hier_moe(x, w_router_group[l], b_router_group[l], w_router_expert[l], b_router_expert[l],
                        w_exp_gate[l], w_exp_up[l], w_exp_down[l])
        x = _layernorm(alpha * x + ffn, ln2_g[l], ln2_b[l])
    return x


def setup_inputs(seed=0):
    out = dict(first_inputs(seed))
    for name, value in second_inputs(seed + 1).items():
        if name != "x":
            out[name + "_2"] = value
    return out


def reference(
    x, c, positions, ada_w, ada_b, norm_mix, norm_ffn, even_w_in, gdn_conv_w, gdn_a_log,
    gdn_dt_bias, gdn_out_norm, even_w_out, gla_w_in, gla_w_gate2, gla_b_gate2, gla_out_norm,
    gla_w_out, router_group_w, router_group_b, router_exp_w, router_exp_b, exp_w1, exp_w3,
    exp_w2, final_norm, positions_2, w_in_2, b_gate_2, b_forget_2, mla_q_norm_2, mla_kv_norm_2,
    mla_w_uq_2, mla_w_ukv_2, conv_w_2, conv_b_2, conv_ln_g_2, conv_ln_b_2, w_branch_2, w_o_2,
    ln1_g_2, ln1_b_2, w_router_group_2, b_router_group_2, w_router_expert_2, b_router_expert_2,
    w_exp_gate_2, w_exp_up_2, w_exp_down_2, ln2_g_2, ln2_b_2,
):
    x = first_block(
        x, c, positions, ada_w, ada_b, norm_mix, norm_ffn, even_w_in, gdn_conv_w, gdn_a_log,
        gdn_dt_bias, gdn_out_norm, even_w_out, gla_w_in, gla_w_gate2, gla_b_gate2, gla_out_norm,
        gla_w_out, router_group_w, router_group_b, router_exp_w, router_exp_b, exp_w1, exp_w3,
        exp_w2, final_norm,
    )
    return second_block(
        x, positions_2, w_in_2, b_gate_2, b_forget_2, mla_q_norm_2, mla_kv_norm_2, mla_w_uq_2,
        mla_w_ukv_2, conv_w_2, conv_b_2, conv_ln_g_2, conv_ln_b_2, w_branch_2, w_o_2, ln1_g_2,
        ln1_b_2, w_router_group_2, b_router_group_2, w_router_expert_2, b_router_expert_2,
        w_exp_gate_2, w_exp_up_2, w_exp_down_2, ln2_g_2, ln2_b_2,
    )


_drawn_inputs = setup_inputs


def setup_inputs(seed=0):
    import zlib

    import numpy as np

    out = dict(_drawn_inputs(seed))
    spreads = {}
    factors = {'norm_mix': 2.814,
     'gdn_dt_bias': 8.0,
     'gdn_out_norm': 6.363,
     'gla_b_gate2': 3.718,
     'gla_out_norm': 8.0,
     'router_group_b': 8.0,
     'router_exp_b': 5.638,
     'b_gate_2': 8.0,
     'b_forget_2': 64.0,
     'mla_q_norm_2': 8.0,
     'mla_kv_norm_2': 8.0,
     'conv_b_2': 5.904,
     'conv_ln_g_2': 7.117,
     'conv_ln_b_2': 8.0,
     'b_router_group_2': 8.0,
     'b_router_expert_2': 7.271}
    for name, (base, spread) in spreads.items():
        noise = np.random.default_rng([zlib.crc32(name.encode()), seed]).standard_normal(out[name].shape)
        drawn = base * np.exp(spread * noise) if base else spread * noise
        out[name] = jnp.asarray(drawn.astype(out[name].dtype))
    for name, factor in factors.items():
        out[name] = (out[name] * factor).astype(out[name].dtype)
    return out
```

```python
from contextlib import ExitStack

import concourse.bass as bass
import concourse.mybir as mybir
import numpy as np

ALU = mybir.AluOpType
ACT = mybir.ActivationFunctionType
F32 = mybir.dt.float32
I32 = mybir.dt.int32
U32 = mybir.dt.uint32
AX = mybir.AxisListType

P = 128
D = 1024
KD = D // P
S = 256
NT = S // P
H = 4
CH = 64
NCH = S // CH
E = 32
NG, EG = 4, 8
CAP = 64
TOPK = 64
CONV1, CONV2 = 4, 31
NR = 6
SLOT = 4096
ALPHA = 4.0 ** 0.25
TAU = 16.0
NEG = -3.0e38
TAKEN = -3.3e38
OFF = -1.0e30
ADA = 6 * D // 512
ADA_FIRST = 2 * D // 512
QA, KA, VA, ZA, BA, QB, KB, VB, QI, KI, WI = 0, 512, 1024, 1536, 2048, 2056, 2568, 3080, 3592, 3848, 3912
MIX2 = dict(cq=0, ckv=256, kr=384, sbq=416, sbv=928, conv=1184, fxq=1696, fxv=2208, ff=2464, gate=2468)



EARLY = ("ones", "small", "quarters", "inv", "c", "norm_mix0", "ada_b0")


def constant_columns():
    i = np.arange(P)
    same = (i[:, None] // CH) == (i[None, :] // CH)
    upper = i[:, None] <= i[None, :]
    keys, q = np.arange(S), np.arange(S)
    causal = np.where(keys[None, :] <= q[:, None], 0.0, NEG)
    strict = np.where(keys[:, None] < q[None, :], 0.0, OFF)

    def rotation(half, heads, width, first=0):
        r = np.zeros((P, P))
        for h in range(heads):
            for j in range(half):
                a, b = first + h * width + j, first + h * width + half + j
                r[a, b], r[b, a] = -1.0, 1.0
        return r.T

    fa = 1.0 / (np.float32(10000.0) ** (np.arange(0, 128, 2, dtype=np.float32) / np.float32(128)))
    fi = 1.0 / (np.float32(10000.0) ** (np.arange(0, 64, 2, dtype=np.float32) / np.float32(64)))
    fm = np.float32(10000.0) ** (-np.arange(16, dtype=np.float32) / np.float32(16))
    inv = np.zeros((P, 3))
    inv[:, 0] = np.tile(fa, 2)
    inv[:, 1] = np.tile(fi, 4)
    inv[64:96, 2] = np.tile(fm, 2)
    half = np.zeros((P, 2, CH))
    for par in range(2):
        half[:, par] = (i[:, None] // CH == par) & (i[:, None] % CH <= np.arange(CH)[None, :])
    c = {
        "ident": np.eye(P),
        "ones": np.ones((P, P)),
        "cum64": (same & upper) * 1.0,
        "all64": same * 1.0,
        "cum": upper * 1.0,
        "ntail": -1.0 * (i[:, None] >= i[None, :]),
        "nones": -np.ones((P, P)),
        "rot_a": rotation(64, 1, 128),
        "rot_i": rotation(32, 2, 64),
        "rot_m": rotation(16, 1, 32, 64),
        "low64": (same & (i[:, None] > i[None, :])) * 1.0,
        "blk16": ((i[:, None] // 16) == (i[None, :] // 16)) * 1.0,
        "off16": ((i[:, None] // 16) != (i[None, :] // 16)) * 1.0,
        "causal": causal.reshape(NT, P, S).transpose(1, 0, 2),
        "strict": np.concatenate([strict[0:P], strict[P:, P:]], 1),
        "half": half,
        "quarters": (i % 32 == 0) * 1.0,
        "zeros": np.zeros((P, P)),
        "par": np.stack([i < CH, i >= CH], 1) * 1.0,
        "run": np.broadcast_to((np.arange(S) % CH != 0) * 1.0, (P, S)),
        "slots": np.broadcast_to(np.arange(1, CAP + 1), (P, CAP)),
        "iota": np.broadcast_to(np.arange(E), (P, E)),
        "inv": inv,
        "small": np.broadcast_to(np.array([1e-6, 1e-5, 1.0, np.log(128.0 ** -0.5), 0.0]), (P, 5)),
    }
    return {k: np.ascontiguousarray(v, np.float32).reshape(P, -1) for k, v in c.items()}


def cols(v):
    return np.asarray(v).reshape(-1, P).T


def rows(v):
    return np.broadcast_to(np.asarray(v).reshape(1, -1), (P, np.asarray(v).size))


def pad(a):
    return np.concatenate([a, np.zeros((P - a.shape[0],) + a.shape[1:], np.float32)], 0)


def router_columns(wg, we):
    w = np.concatenate([wg, we], 1)
    return w.reshape(KD, P, NG + E).transpose(1, 0, 2).reshape(P, -1)


def parameter_columns(a):
    c = {"c": cols(a["c"][0]), "final": cols(a["final_norm"])}
    for l in range(2):
        c[f"ada_b{l}"] = cols(a["ada_b"][l])
        c[f"norm_mix{l}"] = cols(a["norm_mix"][l])
        c[f"norm_ffn{l}"] = cols(a["norm_ffn"][l])
        c[f"rw{l}"] = router_columns(a["router_group_w"][l], a["router_exp_w"][l].transpose(1, 0, 2).reshape(D, E))
        c[f"rb{l}"] = rows(np.concatenate([a["router_group_b"][l], a["router_exp_b"][l].reshape(-1)]))
    c["conv1"] = a["gdn_conv_w"][0].reshape(CONV1, 12, P).transpose(2, 1, 0).reshape(P, -1)
    c["a_log"] = rows(a["gdn_a_log"][0])
    c["dt_bias"] = rows(a["gdn_dt_bias"][0])
    c["gdn_norm"] = cols(a["gdn_out_norm"][0])
    c["gla_w2"] = pad(np.asarray(a["gla_w_gate2"][0]))
    c["gla_b2"] = cols(a["gla_b_gate2"][0])
    c["gla_norm"] = cols(a["gla_out_norm"][0])
    for l in range(2):
        c[f"b_gate_2{l}"] = cols(a["b_gate_2"][l])
        c[f"b_forget_2{l}"] = rows(a["b_forget_2"][l])
        c[f"q_norm_2{l}"] = cols(a["mla_q_norm_2"][l])
        c[f"kv_norm_2{l}"] = cols(a["mla_kv_norm_2"][l])
        c[f"conv2_{l}"] = a["conv_w_2"][l].reshape(CONV2, 2, P).transpose(2, 1, 0).reshape(P, -1)
        for n in ("conv_b_2", "conv_ln_g_2", "conv_ln_b_2", "ln1_g_2", "ln1_b_2", "ln2_g_2", "ln2_b_2"):
            c[f"{n}{l}"] = cols(a[n][l])
        c[f"rw_2{l}"] = router_columns(a["w_router_group_2"][l], a["w_router_expert_2"][l])
        c[f"rb_2{l}"] = rows(np.concatenate([a["b_router_group_2"][l], a["b_router_expert_2"][l]]))
    return {k: np.ascontiguousarray(v, np.float32).reshape(P, -1) for k, v in c.items()}



class Engine:

    def __init__(self, engine):
        self.e = engine
        self.seen, self.loops = {}, []

    def value(self, name):
        base, n = self.seen.setdefault(name, (0, 0))
        return base + n

    def skip(self, name, n=1):
        base, k = self.seen.setdefault(name, (0, 0))
        self.seen[name] = (base, k + n)

    def due(self, name, n=1):
        if self.loops:
            assert name in self.loops[-1][0] or n == 0, f"{name} in a loop"
        self.skip(name, n)
        return self.value(name)

    def enter(self, i, per, start=0):
        saved = {}
        for name, k in per.items():
            base, n = self.seen.setdefault(name, (0, 0))
            saved[name] = (base, n)
            self.seen[name] = ((i - start) * k + (base + n), 0)
        self.loops.append((per, saved))

    def leave(self, passes):
        per, saved = self.loops.pop()
        for name, k in per.items():
            assert self.seen[name][1] == k, (name, self.seen[name][1], k)
            base, n = saved[name]
            self.seen[name] = (base, n + passes * k)


SIGNALS = """
dve_step act_step
inputs_in constants_in moment_ready glr_ready x_ready scaled_ready unit_done lin_read silu_c ada_copied ada_columns ada_read
sq_ready sum_ready rstd_ready norm_ready root_ready var_ready
table_arg table_ready conv_done conv_silu rot_ready rope_ready dots_ready relu_ready keep_ready
logits_ready max_ready exp_ready probs_ready turned turned_read attn_ready attn_read
norms_read gates_ready gate_pre cums_ready decay_pre decay_ready qk_ready qkn_ready
mats_ready scales_ready tri_ready tri_read kv_ready kv_read
state_ready wstate_ready vnew_ready dstate_ready scan_out
mix_ready
gexp_pre gexp_ready gscan_ready gq_ready att_ready att_read
router_ready route_pre route_exp route_done tokens_turned tokens_ready ranks_ready place_ready
gathered xg_ready silu_ready hid_ready hid_turned hidT_ready results_ready gated_ready gated_turned gatedT_ready sum_done
mla_norm sb_pre sb_abs sb_exp sb_soft sb_rev sb_arg sb_prob
fox_pre fox_exp fox_gate fox_cum fox_row convg_ready gate_read
branch_read gts_read gts_ready fill_read
stored
""".split()


def build(nc, a, vec_at, vec_w, out):
    ctx = ExitStack()
    with ctx:
        slab_words = NR * SLOT + vec_w + 2 * KD * S + 2 * S + 18517
        slab = ctx.enter_context(nc.sbuf_tensor("slab", [P, slab_words], F32))
        psum = ctx.enter_context(nc.psum_tensor("psum", [P, 8, 512], F32))
        sems = {n: ctx.enter_context(nc.semaphore(n)) for n in SIGNALS}
        for m in range(4):
            for n in ("step", "column", "row", "loaded", "up", "silu", "hid", "used"):
                sems[f"over_{n}{m}"] = ctx.enter_context(nc.semaphore(f"over_{n}{m}"))
        for s in range(NR):
            sems[f"slot{s}"] = ctx.enter_context(nc.semaphore(f"slot{s}"))

        def view(at, *dims):
            n = int(np.prod(dims))
            assert 0 <= at and at + n <= slab_words, (at, dims, slab_words)
            v = slab[:, at:at + n]
            if len(dims) == 2:
                v = v.rearrange("p (a b) -> p a b", a=dims[0])
            if len(dims) == 3:
                v = v.rearrange("p (a b c) -> p a b c", a=dims[0], b=dims[1])
            return v

        ring = view(0, NR, SLOT)
        VEC = NR * SLOT
        vec = view(VEC, vec_w)
        XO = VEC + vec_w
        xT = view(XO, KD, S)
        HO = XO + KD * S
        hT = view(HO, KD, S)
        cosM, sinM = view(HO + KD * S, S), view(HO + KD * S + S, S)
        AO = HO + KD * S + 2 * S
        AEND = slab_words - 1
        ROOT = view(AEND, 1)

        def v(name, *dims):
            at, n = vec_at[name]
            return view(VEC + at, *(dims or (n,)))

        ident, ones = v("ident"), v("ones")
        small = v("small")
        EPS6, EPS5, ONE, LQ, ZERO = (small[:, j:j + 1] for j in range(5))

        def banks(b, n, *dims):
            r = psum[:, b:b + n, :].rearrange("p a b -> p (a b)")
            m = int(np.prod(dims))
            r = r[:, 0:m]
            if len(dims) == 2:
                r = r.rearrange("p (a b) -> p a b", a=dims[0])
            if len(dims) == 3:
                r = r.rearrange("p (a b c) -> p a b c", a=dims[0], b=dims[1])
            return r

        def over(ap, *dims):
            return ap.unsqueeze(1).broadcast_to([ap.shape[0], *dims, ap.shape[-1]])

        def along(ap, n):
            return ap.unsqueeze(len(ap.shape)).broadcast_to([*ap.shape, n])

        mm = nc.tensor.matmul
        V, A = nc.vector, nc.scalar
        block = ctx.enter_context(nc.Block())

        def kxn(w, c0, n, k=KD):
            return w[:, c0:c0 + n].rearrange("(k p) n -> p k n", p=P)

        def sl(s, k, at=0, n=None):
            w = SLOT // k
            return ring[:, s, :].rearrange("p (k n) -> p k n", k=k)[:, :, at:at + (n or w)]

        def fill_cols(w, c0, n, extra=()):
            def f(s):
                r = [(sl(s, KD, 0, n), kxn(w, c0, n))]
                at = n
                for c, m in extra:
                    r.append((sl(s, KD, at, m), kxn(w, c, m)))
                    at += m
                return r
            return f

        def ada_fills(l):
            return [fill_cols(a["ada_w"][l], 512 * j, 512) for j in range(12)]

        def out_fills(w):
            return [fill_cols(w, 512 * j, 512) for j in range(2)]

        even_w = a["even_w_in"][0]
        even_in_fills = [fill_cols(even_w, QA, 512), fill_cols(even_w, KA, 512), fill_cols(even_w, VA, 512),
                      fill_cols(even_w, QI, 324, ((BA, 8),)), fill_cols(even_w, QB, 512), fill_cols(even_w, KB, 512),
                      fill_cols(even_w, VB, 512), fill_cols(even_w, ZA, 512)]
        even_fills = even_in_fills + ada_fills(0)[ADA_FIRST:] + ada_fills(1) + out_fills(a["even_w_out"][0])
        gla_w = a["gla_w_in"][0]
        gla_fills = [fill_cols(gla_w, 3072, 16)] + [fill_cols(gla_w, 512 * j, 512) for j in range(6)] \
            + out_fills(a["gla_w_out"][0])

        def moe1_fills(l, i):
            def up(w, e):
                return lambda s: [(sl(s, KD), a[w][l, e].rearrange("(k p) n -> p k n", p=P))]

            def down(e):
                return lambda s: [(sl(s, 4), a["exp_w2"][l, e].rearrange("(k p) n -> p k n", p=P))]
            return [up(w, 2 * i + j) for w in ("exp_w1", "exp_w3") for j in range(2)] + [down(2 * i + j) for j in range(2)]

        def moe2_fills(l, i):
            def gate_up(e):
                def f(s):
                    return [(sl(s, KD, 256 * j, 256), a[w][l, e].rearrange("(k p) n -> p k n", p=P))
                            for j, w in enumerate(("w_exp_gate_2", "w_exp_up_2"))]
                return f

            def down(e):
                def f(s):
                    return [(sl(s, 4)[:, 2 * j:2 * j + 2, :],
                             a["w_exp_down_2"][l, e + j].rearrange("(k p) n -> p k n", p=P)) for j in range(2)]
                return f
            return [f for g in range(2) for f in (gate_up(4 * i + 2 * g), gate_up(4 * i + 2 * g + 1), down(4 * i + 2 * g))]

        def mix2_fills(l):
            w = a["w_in_2"][l]

            def ukv(s):
                return [(ring[:, s, 0:768].rearrange("p (k n) -> p k n", k=2),
                         a["mla_w_uq_2"][l].rearrange("(k p) n -> p k n", p=P)),
                        (ring[:, s, 768:1280], a["mla_w_ukv_2"][l])]

            def gate(dc):
                def f(s):
                    return [(sl(s, KD)[:, :, 128 * n:128 * n + 128], kxn(w, MIX2["gate"] + n * D + dc * P, P))
                            for n in range(4)]
                return f

            def branch(j):
                def f(s):
                    return [(sl(s, 4)[:, 2 * i:2 * i + 2, :],
                             a["w_branch_2"][l, 2 * j + i].rearrange("(k p) n -> p k n", p=P)) for i in range(2)]
                return f

            return [fill_cols(w, MIX2["conv"], 512), fill_cols(w, 0, 416, ((MIX2["ff"], 4),)), fill_cols(w, MIX2["sbq"], 512),
                    fill_cols(w, MIX2["sbv"], 256, ((MIX2["fxv"], 256),)), ukv, fill_cols(w, MIX2["fxq"], 512)] \
                + [gate(dc) for dc in range(6)] + [branch(0), branch(1)] + [gate(dc) for dc in range(6, KD)] \
                + out_fills(a["w_o_2"][l])

        ADA_FREE = [j + 1 for j in range(ADA_FIRST)]
        EVEN_FREE = [2, 4, 6, 9, 11, 13, 15, 17] + [18 + j for j in range(2 * ADA - ADA_FIRST)] + [39, 41]
        EVEN_UNITS = 41
        GLA_FREE = [1, 3, 5, 7, 9, 11, 13, 15, 17]
        GLA_UNITS = 17
        MOE1_FREE = [1, 1, 2, 2, 3, 3]
        MOE2_FREE = [1, 1, 2, 3, 3, 4]
        UNITS = {1: 3, 2: 4}
        PASSES = {1: E // 2, 2: E // 4}
        MIX2_FREE = [2, 5, 7, 9, 14, 16, 20, 24, 28, 32, 38, 40, 48, 48, 42, 44, 50, 52]
        MIX2_UNITS = 52

        @block.sync
        def _(sp):
            early = max(sum(vec_at[n]) for n in EARLY)
            sp.dma_start(vec[:, 0:early], a["vec"][:, 0:early]).then_inc(sems["inputs_in"], 16)
            sp.dma_start(xT, a["xT"].rearrange("(k p) n -> p k n", p=P)).then_inc(sems["inputs_in"], 16)
            at = [0, 0, [None] * NR]

            def fill(f, free):
                s = at[0] % NR
                if at[2][s] is not None:
                    sp.wait_ge(sems["unit_done"], at[2][s])
                for dst, src in f(s):
                    sp.dma_start(dst, src).then_inc(sems[f"slot{s}"], 16)
                at[2][s] = free
                at[0] += 1

            def phase(fills, free, units):
                for f, u in zip(fills, free):
                    fill(f, at[1] + u)
                at[1] += units

            def experts(l, kind, pass_fills, free):
                first, units, passes = at[1], UNITS[kind], PASSES[kind]
                for f, u in zip(pass_fills(l, 0), free):
                    fill(f, first + u)
                with sp.Fori(1, passes) as i:
                    for j, f in enumerate(pass_fills(l, i)):
                        s = (at[0] + j) % NR
                        sp.wait_ge(sems["unit_done"], (i - 1) * units + (first + free[j]))
                        for dst, src in f(s):
                            sp.dma_start(dst, src).then_inc(sems[f"slot{s}"], 16)
                at[1] = first + passes * units
                for j in range(6):
                    at[2][(at[0] + j) % NR] = at[1] - units + free[j]

            for l in range(2):
                if l == 0:
                    phase(ada_fills(0)[:ADA_FIRST], ADA_FREE, ADA_FIRST)
                    phase(even_fills[0:2], EVEN_FREE[0:2], 0)
                    sp.dma_start(vec[:, early:], a["vec"][:, early:]).then_inc(sems["constants_in"], 16)
                    phase(even_fills[2:], EVEN_FREE[2:], EVEN_UNITS)
                else:
                    phase(gla_fills, GLA_FREE, GLA_UNITS)
                experts(l, 1, moe1_fills, MOE1_FREE)
            for l in range(2):
                phase(mix2_fills(l), MIX2_FREE, MIX2_UNITS)
                experts(l, 2, moe2_fills, MOE2_FREE)
            norms, half = 5 + 4, KD // 2
            for n in range(2):
                sp.wait_ge(sems["norm_ready"], (norms - 1) * KD + half * (n + 1))
                sp.dma_start(out[half * P * n:half * P * n + half * P, :].rearrange("(k p) n -> p k n", p=P),
                             xT[:, half * n:half * n + half, :]).then_inc(sems["stored"], 16)
            sp.wait_ge(sems["stored"], 32)

        PER = AO
        modc = view(PER, 48)
        coef = view(PER + 48, KD)
        silc = view(PER + 56, KD)
        s12 = view(PER + 64, NT, 12)
        mod_raw = view(PER + 96, 2, 48)
        gsm = view(PER + 192, 12, NT * H)
        rstd = view(PER + 288, 2, S)
        A0 = PER + 288 + 2 * S

        def slot(q, dmas=1):
            s = q.slot % NR
            q.slot += 1
            q.e.wait_ge(sems[f"slot{s}"], q.due(f"slot{s}", 16 * dmas))
            return s

        def accumulate(out_ap, pairs):
            for n, (lhs, rhs) in enumerate(pairs):
                ins = mm(out_ap, lhs, rhs, start=(n == 0), stop=(n == len(pairs) - 1), skip_group_check=True)
            return ins

        class Units:

            def __init__(self, q):
                self.q, self.n, self.read = q, 0, 0

            def need(self, n):
                q = self.q
                if n > self.read:
                    q.e.wait_ge(sems["lin_read"], q.due("lin_read", n - self.read))
                    self.read = n

            def bank(self):
                self.need(self.n - 3)
                self.n += 1
                return (self.n - 1) % 4

            def end(self):
                self.need(self.n)

        def pe_features(u, s, src, c0, first=None):
            b = u.bank()
            for j in range(2):
                for k in range(KD):
                    if first is not None and j == 0:
                        q = first
                        q.e.wait_ge(sems["norm_ready"], q.due("norm_ready"))
                    ins = mm(psum[:, b, S * j:S * j + S], sl(s, KD)[:, k, c0 + P * j:c0 + P * j + P], src[:, k, :],
                             start=(k == 0), stop=(k == KD - 1), skip_group_check=True)
            ins.then_inc(sems["unit_done"], 1)

        def pe_tokens(u, s, src, c0, n, tile, k=KD):
            b = u.bank()
            accumulate(psum[:, b, 0:n], [(src[:, i, P * tile:P * tile + P], sl(s, k)[:, i, c0:c0 + n])
                                         for i in range(k)]).then_inc(sems["unit_done"], 1)

        def act_unit(q, b, dst, func=ACT.Copy, n=512, shape=None, **kw):
            q.e.wait_ge(sems["unit_done"], q.due("unit_done"))
            src = psum[:, b % 4, 0:n]
            if shape is not None:
                src = src.rearrange("p (a b) -> p a b", a=shape)
            return A.activation(dst, src, func, **kw).then_inc(sems["lin_read"], 1)

        NSQ = view(A0 + 3200, KD, S)

        def act_squares(q, dst, wait=True):
            for b in range(KD // 2):
                if wait:
                    q.e.wait_ge(sems["x_ready"], q.due("x_ready"))
                c = slice(2 * b, 2 * b + 2)
                A.activation(dst[:, c, :], xT[:, c, :], ACT.Square, scale=D ** -0.5).then_inc(sems["sq_ready"], 1)
            act_root_table(q)

        def pe_square_sum(q, sq, bank, mean=False):
            for k in range(KD):
                if k % 2 == 0:
                    q.e.wait_ge(sems["sq_ready"], q.due("sq_ready"))
                if mean:
                    mm(psum[:, bank + 1, 0:S], ones, xT[:, k, :], start=(k == 0), stop=(k == KD - 1), skip_group_check=True)
                ins = mm(psum[:, bank, 0:S], ones, sq[:, k, :], start=(k == 0), stop=(k == KD - 1), skip_group_check=True)
            ins.then_inc(sems["moment_ready"], 1)

        def act_root_table(q):
            A.activation(ROOT, ONE, ACT.Sqrt)

        def act_root(q, dst, src):
            q.e.wait_ge(sems["moment_ready"], q.due("moment_ready"))
            A.activation(dst, src, ACT.Sqrt, bias=EPS6).then_inc(sems["root_ready"], 1)

        def dve_norm(q, gain, dst, done):
            q.e.wait_ge(sems["root_ready"], q.due("root_ready"))
            q.skip("moment_ready")
            V.reciprocal(rstd[:, 0, :], rstd[:, 0, :]).then_inc(sems["dve_step"], 1)
            q.e.wait_ge(sems["dve_step"], q.due("dve_step"))
            for k in range(KD):
                V.scalar_tensor_tensor(out=dst[:, k, :], in0=xT[:, k, :], scalar=gain[:, k:k + 1], in1=rstd[:, 0, :],
                                       op0=ALU.mult, op1=ALU.mult).then_inc(sems[done], 1)

        def act_shift(q, dst, shift):
            for k in range(KD):
                q.e.wait_ge(sems["scaled_ready"], q.due("scaled_ready"))
                A.activation(dst[:, k, :], dst[:, k, :], ACT.Identity, bias=shift[:, k:k + 1]).then_inc(sems["norm_ready"], 1)

        def pe_ada_rows(q, bank):
            s = slot(q)
            for r in range(KD // 4):
                for g in range(4):
                    k = 4 * r + g
                    ins = mm(psum[32 * g:32 * g + 32, bank, :], silc[:, k:k + 1].broadcast_to([P, 32]), sl(s, KD)[:, k, :],
                             start=(r == 0), stop=(r == KD // 4 - 1), skip_group_check=True)
            ins.then_inc(sems["unit_done"], 1)

        def pe_ada_columns(q, j, bank):
            q.e.wait_ge(sems["ada_copied"], q.due("ada_copied"))
            for n in range(4):
                ins = mm(psum[:, bank, n:n + 1], ada_rows[:, j % 2, P * n:P * n + P], v("quarters"), start=True, stop=True)
            ins.then_inc(sems["ada_columns"], 1)

        def act_ada_rows(q, j, bank):
            q.e.wait_ge(sems["unit_done"], q.due("unit_done"))
            A.activation(ada_rows[:, j % 2, :], psum[:, bank, :], ACT.Copy).then_inc(sems["ada_copied"], 1)

        def act_ada_columns(q, j, bank):
            q.e.wait_ge(sems["ada_columns"], q.due("ada_columns"))
            A.activation(mod_raw[:, j // ADA, 4 * (j % ADA):4 * (j % ADA) + 4], psum[:, bank, 0:4], ACT.Copy)\
                .then_inc(sems["ada_read"], 1)

        def pe_ada_need(q, n):
            if n > q.ada_read:
                q.e.wait_ge(sems["ada_read"], q.due("ada_read", n - q.ada_read))
                q.ada_read = n

        def pe_ada(q, steps, b):
            for _ in range(steps):
                if q.ada_bank is not None:
                    pe_ada_columns(q, q.ada - 1, q.ada_bank)
                pe_ada_need(q, q.ada - 1)
                q.ada_bank = b + q.ada % 2
                pe_ada_rows(q, q.ada_bank)
                q.ada += 1

        def pe_ada_end(q):
            pe_ada_columns(q, q.ada - 1, q.ada_bank)
            q.ada_bank = None
            pe_ada_need(q, q.ada)

        def act_ada(q, steps, b):
            for _ in range(steps):
                if q.ada_bank is not None:
                    act_ada_columns(q, q.ada - 1, q.ada_bank)
                q.ada_bank = b + q.ada % 2
                act_ada_rows(q, q.ada, q.ada_bank)
                q.ada += 1

        def act_ada_end(q):
            act_ada_columns(q, q.ada - 1, q.ada_bank)
            q.ada_bank = None

        def dve_ada(q, l, steps, first, last):
            q.e.wait_ge(sems["ada_read"], q.due("ada_read", steps))
            V.tensor_tensor(modc[:, first:last], mod_raw[:, l, first:last], v(f"ada_b{l}")[:, first:last], ALU.add).then_inc(sems["dve_step"], 1)
            q.e.wait_ge(sems["dve_step"], q.due("dve_step"))

        def dve_coef(q, half, gain):
            V.scalar_tensor_tensor(out=coef, in0=modc[:, 24 * half + 8:24 * half + 16], scalar=1.0, in1=gain,
                                   op0=ALU.add, op1=ALU.mult).then_inc(sems["dve_step"], 1)
            q.e.wait_ge(sems["dve_step"], q.due("dve_step"))

        def pe_out(q, src, early, late, out_banks):
            w = [slot(q), slot(q)]
            for part in (early, late):
                if part is late:
                    q.e.wait_ge(sems["mix_ready"], q.due("mix_ready"))
                for n, b in enumerate(out_banks):
                    for j in range(2):
                        c0 = P * (2 * (n % 2) + j)
                        for k in part:
                            ins = mm(psum[:, b, S * j:S * j + S], sl(w[n // 2], KD)[:, k, c0:c0 + P], src[:, k, :],
                                     start=(part is early and j == 0 and k == early[0]),
                                     stop=(part is late and j == 1 and k == late[-1]), skip_group_check=True)
                    if part is late:
                        ins.then_inc(sems["unit_done"], 1)

        def dve_residual(q, gate0, out_banks):
            for b, bank in enumerate(out_banks):
                q.e.wait_ge(sems["unit_done"], q.due("unit_done"))
                for j in range(2):
                    k = 2 * b + j
                    ins = V.scalar_tensor_tensor(out=xT[:, k, :], in0=psum[:, bank, S * j:S * j + S],
                                                 scalar=modc[:, gate0 + k:gate0 + k + 1], in1=xT[:, k, :],
                                                 op0=ALU.mult, op1=ALU.add)
                ins.then_inc(sems["x_ready"], 1)
            q.e.wait_ge(sems["x_ready"], q.due("x_ready", 4))

        class Attention:

            def __init__(self, at, order, scale, turn=4):
                self.lg = view(at, NT, H, S)
                self.pT = view(at + 2048, H, 3, P)
                self.nmax, self.sums = view(at + 3584, NT, H), view(at + 3592, NT, H)
                self.order, self.scale, self.turn = order, scale, turn

            def pe_logits(self, q, qk):
                for t in range(NT):
                    for j in range(H):
                        lhs, rhs = qk(j, t)
                        ins = mm(psum[:, 2 * t + j // 2, S * (j % 2):S * (j % 2) + S], lhs, rhs, start=True, stop=True)
                    ins.then_inc(sems["logits_ready"], 1)

            def dve_max(self, q, t, bias, op=ALU.add):
                q.e.wait_ge(sems["logits_ready"], q.due("logits_ready"))
                lg = self.lg[:, t]
                V.scalar_tensor_tensor(out=lg, in0=banks(2 * t, 2, H, S), scalar=self.scale, in1=bias,
                                       op0=ALU.mult, op1=op).then_inc(sems["dve_step"], 1)
                q.e.wait_ge(sems["dve_step"], q.due("dve_step"))
                V.tensor_reduce(self.nmax[:, t, :], lg, AX.X, ALU.max, negate=True).then_inc(sems["max_ready"], 1)

            def act_exp(self, q, t):
                q.e.wait_ge(sems["max_ready"], q.due("max_ready"))
                for j in range(H):
                    ins = A.activation(self.lg[:, t, j, :], self.lg[:, t, j, :], ACT.Exp,
                                       bias=self.nmax[:, t, j:j + 1], accum_out=self.sums[:, t, j:j + 1])
                ins.then_inc(sems["exp_ready"], 1)

            def dve_probs(self, q, t):
                q.e.wait_ge(sems["exp_ready"], q.due("exp_ready"))
                V.reciprocal(self.sums[:, t, :], self.sums[:, t, :]).then_inc(sems["dve_step"], 1)
                q.e.wait_ge(sems["dve_step"], q.due("dve_step"))
                V.tensor_tensor(self.lg[:, t], self.lg[:, t], along(self.sums[:, t, :], S), ALU.mult)\
                    .then_inc(sems["probs_ready"], 1)

            def pe_turn(self, q):
                turned = banks(self.turn, 3, H, 3, P)
                for t in range(NT):
                    q.e.wait_ge(sems["probs_ready"], q.due("probs_ready"))
                    for j in range(H):
                        for kt in range(t + 1):
                            ins = nc.tensor.transpose(turned[:, j, t + kt, :], self.lg[:, t, j, P * kt:P * kt + P], ident)
                ins.then_inc(sems["turned"], 1)

            def act_turned(self, q):
                q.e.wait_ge(sems["turned"], q.due("turned"))
                A.activation(self.pT, banks(self.turn, 3, H, 3, P), ACT.Copy).then_inc(sems["turned_read"], 1)

            def pe_values(self, q, v_of, out_of):
                q.e.wait_ge(sems["turned_read"], q.due("turned_read"))
                for j in range(H):
                    h = self.order[j]
                    o = out_of(h)
                    mm(o, v_of(h, 0), self.pT[:, j, 0:2, :].rearrange("p a b -> p (a b)"), start=True, stop=False,
                       skip_group_check=True)
                    ins = mm(o[:, P:S], v_of(h, 1), self.pT[:, j, 2, :], start=False, stop=True, skip_group_check=True)
                ins.then_inc(sems["attn_ready"], 1)

        TWO_PI = 2.0 * np.pi
        C1 = 6.28125
        C2 = float(TWO_PI - C1)
        ROUND = 1.5 * 2.0 ** 23
        PI = 3.1415925

        pre = view(A0, 12, S + 3)
        cv = view(A0 + 3108, 12, S)
        zs = view(A0 + 6180, H, S)
        mix = view(A0 + 7204, KD, S)
        ada_rows = view(A0 + 7204, 2, 512)
        R0 = A0 + 9252
        qb, kb = view(R0, H, S), view(R0 + 1024, H, S)
        vb = view(R0 + 2048, NT, 512)
        qi, ki = view(R0 + 3072, 2, S), view(R0 + 3584, S)
        cosA, sinA, cosI, sinI = (view(R0 + 3840 + S * j, S) for j in range(4))
        W0 = R0 + 4864
        tab_pos = view(A0, 2, S).bitcast(I32)
        tab_f = view(A0 + 512, 2, S)
        tab_k, tab_r = view(A0 + 1024, S), view(A0 + 1280, S)
        tab_arg = view(A0 + 1536, 3, 2, S)

        def dve_tables(q):
            inv = v("inv")
            V.tensor_copy(tab_f, tab_pos).then_inc(sems["dve_step"], 1)
            q.e.wait_ge(sems["dve_step"], q.due("dve_step"))
            for j, pos in ((0, 0), (1, 0), (2, 1)):
                V.tensor_scalar(tab_r, tab_f[:, pos, :], inv[:, j:j + 1], None, ALU.mult).then_inc(sems["dve_step"], 1)
                q.e.wait_ge(sems["dve_step"], q.due("dve_step"))
                V.tensor_scalar(tab_k, tab_r, 1.0 / TWO_PI, ROUND, ALU.mult, ALU.add).then_inc(sems["dve_step"], 1)
                q.e.wait_ge(sems["dve_step"], q.due("dve_step"))
                V.tensor_scalar(tab_k, tab_k, ROUND, None, ALU.subtract).then_inc(sems["dve_step"], 1)
                q.e.wait_ge(sems["dve_step"], q.due("dve_step"))
                V.scalar_tensor_tensor(out=tab_r, in0=tab_k, scalar=-C1, in1=tab_r, op0=ALU.mult, op1=ALU.add).then_inc(sems["dve_step"], 1)
                q.e.wait_ge(sems["dve_step"], q.due("dve_step"))
                V.scalar_tensor_tensor(out=tab_r, in0=tab_k, scalar=-C2, in1=tab_r, op0=ALU.mult, op1=ALU.add).then_inc(sems["dve_step"], 1)
                q.e.wait_ge(sems["dve_step"], q.due("dve_step"))
                V.tensor_scalar(tab_arg[:, j, 0, :], tab_r, PI, -PI, ALU.min, ALU.max)
                V.tensor_scalar(tab_r, tab_r, np.pi / 2, None, ALU.add).then_inc(sems["dve_step"], 1)
                q.e.wait_ge(sems["dve_step"], q.due("dve_step"))
                V.tensor_scalar(tab_k, tab_r, PI, -TWO_PI, ALU.is_gt, ALU.mult).then_inc(sems["dve_step"], 1)
                q.e.wait_ge(sems["dve_step"], q.due("dve_step"))
                V.tensor_tensor(tab_r, tab_r, tab_k, ALU.add).then_inc(sems["dve_step"], 1)
                q.e.wait_ge(sems["dve_step"], q.due("dve_step"))
                ins = V.tensor_scalar(tab_arg[:, j, 1, :], tab_r, PI, -PI, ALU.min, ALU.max)
                if j < 2:
                    ins.then_inc(sems["dve_step"], 1)
                    q.e.wait_ge(sems["dve_step"], q.due("dve_step"))
            ins.then_inc(sems["table_arg"], 1)

        def act_tables(q):
            q.e.wait_ge(sems["table_arg"], q.due("table_arg"))
            for j, (c, s) in enumerate(((cosA, sinA), (cosI, sinI), (cosM, sinM))):
                A.activation(s, tab_arg[:, j, 0, :], ACT.Sin)
                ins = A.activation(c, tab_arg[:, j, 1, :], ACT.Sin)
            ins.then_inc(sems["table_ready"], 1)

        def pe_even_in(q):
            u = Units(q)
            for j in range(3):
                s = slot(q)
                for n in range(2):
                    pe_features(u, s, hT, 2 * P * n, q if j + n == 0 else None)
            q.e.wait_ge(sems["constants_in"], q.due("constants_in", 16))
            s = slot(q, 2)
            pe_features(u, s, hT, 0)
            b = u.bank()
            for half in range(2):
                ins = accumulate(psum[CH * half:CH * half + CH, b, 0:S],
                                 [(sl(s, KD)[:, k, 256:320], hT[:, k, :]) for k in range(KD)])
            ins.then_inc(sems["unit_done"], 1)
            b = u.bank()
            for t in range(NT):
                ins = accumulate(psum[:, b, 12 * t:12 * t + 12],
                                 [(hT[:, k, P * t:P * t + P], sl(s, KD)[:, k, 320:332]) for k in range(KD)])
            ins.then_inc(sems["unit_done"], 1)
            for j in range(2):
                s = slot(q)
                for n in range(2):
                    pe_features(u, s, hT, 2 * P * n)
            pe_delta_norm(q)
            s = slot(q)
            for t in range(NT):
                pe_tokens(u, s, hT, 0, 512, t)
            s = slot(q)
            for n in range(2):
                pe_features(u, s, hT, 2 * P * n)
            u.end()

        def act_even_in(q):
            n = 0
            for j in range(6):
                act_unit(q, n, pre[:, 2 * j:2 * j + 2, 3:3 + S], shape=2)
                n += 1
            act_unit(q, n, qi, shape=2)
            act_unit(q, n + 1, ki, n=S)
            act_unit(q, n + 2, s12, n=24, shape=2)
            n += 3
            act_gates(q)
            for dst in (qb, kb):
                for j in range(2):
                    act_unit(q, n, dst[:, 2 * j:2 * j + 2, :], shape=2)
                    n += 1
                if dst is qb:
                    q.e.wait_ge(sems["conv_done"], q.due("conv_done"))
                    A.activation(cv, cv, ACT.Silu).then_inc(sems["conv_silu"], 1)
                    q.e.wait_ge(sems["conv_silu"], q.due("conv_silu"))
                    act_delta_norm(q)
            act_delta_norm2(q)
            for t in range(NT):
                act_unit(q, n, vb[:, t, :])
                n += 1
            for j in range(2):
                act_unit(q, n, zs[:, 2 * j:2 * j + 2, :], ACT.Silu, shape=2)
                n += 1

        def dve_conv(q):
            w = v("conv1", 12, CONV1)
            for j in range(CONV1):
                for c in range(12):
                    x = pre[:, c, j:j + S]
                    if j == 0:
                        ins = V.tensor_scalar(cv[:, c, :], x, w[:, c, 0:1], None, ALU.mult)
                    else:
                        ins = V.scalar_tensor_tensor(out=cv[:, c, :], in0=x, scalar=w[:, c, j:j + 1], in1=cv[:, c, :],
                                                     op0=ALU.mult, op1=ALU.add)
                if j < CONV1 - 1:
                    ins.then_inc(sems["dve_step"], 1)
                    q.e.wait_ge(sems["dve_step"], q.due("dve_step"))
            ins.then_inc(sems["conv_done"], 1)

        t1 = view(A0, 4, S)
        relu = view(A0, H, S)
        sa = Attention(W0, range(H), 128.0 ** -0.5, 0)
        score, work = view(A0 + 1024, S), view(A0 + 1280, S)
        best = view(A0 + 1536, 8)
        keep = view(A0 + 1600, NT, S)

        def pe_rope(q):
            q.e.wait_ge(sems["norms_read"], q.due("norms_read"))
            for n, x in enumerate((qb, kb)):
                for j in range(2):
                    ins = mm(psum[:, 2 * n + j, :], v("rot_a"), x[:, 2 * j:2 * j + 2, :].rearrange("p a b -> p (a b)"),
                             start=True, stop=True)
            mm(psum[:, 4, :], v("rot_i"), qi.rearrange("p a b -> p (a b)"), start=True, stop=True)
            mm(psum[:, 5, 0:S], v("rot_i"), ki, start=True, stop=True).then_inc(sems["rot_ready"], 1)

        def dve_rope(q):
            q.e.wait_ge(sems["lin_read"], q.due("lin_read", 8))
            q.e.wait_ge(sems["rot_ready"], q.due("rot_ready"))
            q.e.wait_ge(sems["conv_done"], q.due("conv_done"))
            for x, r, c, s, n in ((qb, banks(0, 2, H, S), cosA, sinA, H), (kb, banks(2, 2, H, S), cosA, sinA, H),
                                  (qi, banks(4, 1, 2, S), cosI, sinI, 2), (ki.unsqueeze(1), banks(5, 1, 1, S), cosI, sinI, 1)):
                V.tensor_tensor(t1[:, 0:n, :], r, over(s, n), ALU.mult)
                V.tensor_tensor(x, x, over(c, n), ALU.mult).then_inc(sems["dve_step"], 1)
                q.e.wait_ge(sems["dve_step"], q.due("dve_step"))
                ins = V.tensor_tensor(x, x, t1[:, 0:n, :], ALU.add)
                if n > 1:
                    ins.then_inc(sems["dve_step"], 1)
                    q.e.wait_ge(sems["dve_step"], q.due("dve_step"))
            ins.then_inc(sems["rope_ready"], 1)

        def pe_dots(q):
            q.e.wait_ge(sems["rope_ready"], q.due("rope_ready"))
            for t in range(NT):
                for h in range(H):
                    half = CH * (h % 2)
                    ins = mm(psum[:, 4 + 2 * t + h % 2, S * (h // 2):S * (h // 2) + S],
                             qi[half:half + CH, h // 2, P * t:P * t + P], ki[half:half + CH, :], start=True, stop=True)
                ins.then_inc(sems["dots_ready"], 1)

        def act_relu(q):
            for t in range(NT):
                q.e.wait_ge(sems["dots_ready"], q.due("dots_ready"))
                if t > 0:
                    q.e.wait_ge(sems["keep_ready"], q.due("keep_ready"))
                A.activation(relu, banks(4 + 2 * t, 2, H, S), ACT.Relu, scale=1.0).then_inc(sems["relu_ready"], 1)

        def dve_keep(q, t):
            q.e.wait_ge(sems["relu_ready"], q.due("relu_ready"))
            for n, h in enumerate((0, 2, 1, 3)):
                w = s12[:, t, h:h + 1]
                if n == 0:
                    V.tensor_scalar(score, relu[:, n, :], w, None, ALU.mult).then_inc(sems["dve_step"], 1)
                    q.e.wait_ge(sems["dve_step"], q.due("dve_step"))
                else:
                    V.scalar_tensor_tensor(out=score, in0=relu[:, n, :], scalar=w, in1=score,
                                           op0=ALU.mult, op1=ALU.add).then_inc(sems["dve_step"], 1)
                    q.e.wait_ge(sems["dve_step"], q.due("dve_step"))
            causal = v("causal", NT, S)[:, t, :]
            ins = V.scalar_tensor_tensor(out=work, in0=score, scalar=(H * 64.0) ** -0.5, in1=causal,
                                         op0=ALU.mult, op1=ALU.add)
            ins.then_inc(sems["keep_ready"], 1)
            q.e.wait_ge(sems["keep_ready"], q.due("keep_ready"))
            for n in range(TOPK // 8):
                V.max(best, work).then_inc(sems["dve_step"], 1)
                q.e.wait_ge(sems["dve_step"], q.due("dve_step"))
                V.match_replace(work, best, work, TAKEN).then_inc(sems["dve_step"], 1)
                q.e.wait_ge(sems["dve_step"], q.due("dve_step"))
            V.tensor_scalar(keep[:, t, :], work, (NEG + TAKEN) / 2, OFF, ALU.is_gt, ALU.mult).then_inc(sems["dve_step"], 1)
            q.e.wait_ge(sems["dve_step"], q.due("dve_step"))
            return V.tensor_tensor(keep[:, t, :], keep[:, t, :], causal, ALU.add)

        ADA_STEPS = (3, 5, 5, 3, 4)

        def pe_sparse(q):
            pe_ada(q, ADA_STEPS[0], 6)
            pe_ada_end(q)
            pe_dots(q)
            sa.pe_logits(q, lambda j, t: (qb[:, j, P * t:P * t + P], kb[:, j, :]))
            q.e.wait_ge(sems["relu_ready"], q.due("relu_ready", 2))
            pe_ada(q, ADA_STEPS[1], 4)
            pe_ada_end(q)
            pe_decay(q)
            sa.pe_turn(q)
            sa.pe_values(q, lambda h, t: vb[:, t, P * h:P * h + P], lambda h: banks(6, 2, H, S)[:, h, :])

        def act_sparse(q):
            act_ada(q, ADA_STEPS[0], 6)
            act_ada_end(q)
            act_relu(q)
            act_ada(q, ADA_STEPS[1], 4)
            act_ada_end(q)
            for t in range(NT):
                sa.act_exp(q, t)
            act_decay(q)
            sa.act_turned(q)
            q.e.wait_ge(sems["attn_ready"], q.due("attn_ready"))
            A.activation(mix[:, 4:8, :], banks(6, 2, H, S), ACT.Copy).then_inc(sems["attn_read"], 1)

        def dve_sparse(q):
            for t in range(NT):
                dve_keep(q, t).then_inc(sems["dve_step"], 1)
                q.e.wait_ge(sems["dve_step"], q.due("dve_step"))
            for t in range(NT):
                sa.dve_max(q, t, over(keep[:, t, :], H))
            dve_decay2(q)
            for t in range(NT):
                sa.dve_probs(q, t)

        TH = NT * H
        egrow = view(R0, H, S)
        decT = view(HO, TH, P)
        decN = view(HO + 1024, TH, P)
        kd = view(R0 + 3072, 2, TH, P)
        nsq = view(W0, 2 * H, S)
        osq = view(R0 + 3072, 2 * H, S)
        kv = view(R0 + 5120, TH, 2 * P)
        Sst = view(R0 + 7168, H, P)
        vnew = view(R0 + 7680, H, P)
        Pt = view(A0, TH, P)
        Lt = view(A0 + 1024, TH, P)
        Em = view(A0 + 2048, TH, P)
        wT = Em
        L2, Lt2 = view(R0 + 1024, TH, P), view(R0 + 2048, TH, P)
        L4, Lt4 = decN, Lt
        L8, Fm = L2, Lt2
        Ft, Ft2 = L4, Lt4
        beta, gl_, cN, lN, bg, dl0, dl1, g1, g2, g3, ea = (gsm[:, j, :] for j in range(11))

        def th(x, t, h):
            return x[:, t * H + h, :]

        def act_delta_norm(q):
            A.activation(nsq, cv[:, 0:8, :], ACT.Square).then_inc(sems["sq_ready"], 1)

        def pe_delta_norm(q):
            q.e.wait_ge(sems["sq_ready"], q.due("sq_ready"))
            for j in range(4):
                ins = mm(psum[:, 4 + j, :], ones, nsq[:, 2 * j:2 * j + 2, :].rearrange("p a b -> p (a b)"), start=True, stop=True)
            ins.then_inc(sems["sum_ready"], 1)

        def act_delta_norm2(q):
            q.e.wait_ge(sems["sum_ready"], q.due("sum_ready"))
            A.activation(nsq, banks(4, 4, 2 * H, S), ACT.Ln, bias=EPS6).then_inc(sems["norms_read"], 1)
            q.e.wait_ge(sems["norms_read"], q.due("norms_read"))
            A.activation(nsq[:, 0:H, :], nsq[:, 0:H, :], ACT.Exp, scale=-0.5, bias=LQ)
            A.activation(nsq[:, H:, :], nsq[:, H:, :], ACT.Exp, scale=-0.5, bias=ZERO).then_inc(sems["rstd_ready"], 1)

        def dve_gates(q):
            q.e.wait_ge(sems["lin_read"], q.due("lin_read", 9))
            V.tensor_copy(beta.rearrange("p (t h) -> p t h", t=NT), s12[:, :, 4:8])
            V.tensor_tensor(g1.rearrange("p (t h) -> p t h", t=NT), s12[:, :, 8:12], over(v("dt_bias"), NT), ALU.add).then_inc(sems["dve_step"], 1)
            q.e.wait_ge(sems["dve_step"], q.due("dve_step"))
            V.scalar_tensor_tensor(out=g2, in0=g1, scalar=-1.0, in1=g1, op0=ALU.mult, op1=ALU.max).then_inc(sems["dve_step"], 1)
            q.e.wait_ge(sems["dve_step"], q.due("dve_step"))
            V.tensor_scalar(g1, g1, 0.0, None, ALU.max).then_inc(sems["gate_pre"], 1)

        def act_gates(q):
            q.e.wait_ge(sems["gate_pre"], q.due("gate_pre"))
            A.activation(beta, beta, ACT.Sigmoid)
            A.activation(g3, g2, ACT.Exp, scale=-1.0).then_inc(sems["act_step"], 1)
            q.e.wait_ge(sems["act_step"], q.due("act_step"))
            A.activation(g3, g3, ACT.Ln, bias=ONE)
            A.activation(ea[:, 0:H], v("a_log"), ACT.Exp).then_inc(sems["gates_ready"], 1)

        def dve_decay(q):
            q.e.wait_ge(sems["gates_ready"], q.due("gates_ready"))
            V.tensor_tensor(g1, g1, g3, ALU.add).then_inc(sems["dve_step"], 1)
            q.e.wait_ge(sems["dve_step"], q.due("dve_step"))
            V.scalar_tensor_tensor(out=gl_.rearrange("p (t h) -> p t h", t=NT), in0=g1.rearrange("p (t h) -> p t h", t=NT),
                                   scalar=-1.0, in1=over(ea[:, 0:H], NT), op0=ALU.mult, op1=ALU.mult)\
                .then_inc(sems["gate_pre"], 1)

        def pe_decay(q):
            q.e.wait_ge(sems["gate_pre"], q.due("gate_pre", 2))
            for t in range(NT):
                g = gl_[:, t * H:t * H + H]
                mm(psum[:, 6, t * H:t * H + H], v("cum64"), g, start=True, stop=True)
                mm(psum[:, 6, TH + t * H:TH + t * H + H], v("all64"), g, start=True, stop=True)
            for h in range(H):
                for t in range(NT):
                    ins = mm(banks(4, 2, H, S)[:, h, P * t:P * t + P],
                             gl_[:, t * H + h:t * H + h + 1].broadcast_to([P, P]), v("cum64"), start=True, stop=True)
            ins.then_inc(sems["cums_ready"], 1)

        def dve_decay2(q):
            q.e.wait_ge(sems["cums_ready"], q.due("cums_ready"))
            V.tensor_copy(lN, psum[:, 6, TH:2 * TH])
            V.tensor_copy(cN, psum[:, 6, 0:TH]).then_inc(sems["dve_step"], 1)
            q.e.wait_ge(sems["dve_step"], q.due("dve_step"))
            crow = banks(4, 2, H, S)
            for t in range(NT):
                for h in range(H):
                    c, x = cN[:, t * H + h:t * H + h + 1], crow[:, h, P * t:P * t + P]
                    V.tensor_scalar(th(decT, t, h), x, c, 0.0, ALU.subtract, ALU.min)
                    V.tensor_scalar(th(decN, t, h), x, c, 0.0, ALU.subtract, ALU.max)
            V.tensor_tensor(lN, lN, cN, ALU.subtract).then_inc(sems["decay_pre"], 1)

        def act_decay(q):
            q.e.wait_ge(sems["decay_pre"], q.due("decay_pre"))
            A.activation(egrow, banks(4, 2, H, S), ACT.Exp)
            A.activation(decT, decT, ACT.Exp)
            A.activation(decN, decN, ACT.Exp, scale=-1.0)
            A.activation(bg, cN, ACT.Exp)
            A.activation(lN, lN, ACT.Exp).then_inc(sems["decay_ready"], 1)

        def dve_qk(q):
            q.e.wait_ge(sems["conv_silu"], q.due("conv_silu"))
            q.e.wait_ge(sems["rstd_ready"], q.due("rstd_ready"))
            V.tensor_tensor(cv[:, 0:8, :], cv[:, 0:8, :], nsq, ALU.mult).then_inc(sems["qkn_ready"], 1)

        def dve_scales(q):
            q.e.wait_ge(sems["decay_ready"], q.due("decay_ready"))
            V.tensor_tensor(decT, decT, over(v("cum64"), TH), ALU.mult)
            V.tensor_tensor(decN, decN, over(v("low64"), TH), ALU.mult)
            V.tensor_tensor(bg, bg, beta, ALU.mult)
            V.tensor_scalar(dl0, lN, v("par")[:, 0:1], None, ALU.mult)
            V.tensor_scalar(dl1, lN, v("par")[:, 1:2], None, ALU.mult).then_inc(sems["scales_ready"], 1)
            q.e.wait_ge(sems["scales_ready"], q.due("scales_ready"))

        def pe_qk(q):
            q.e.wait_ge(sems["qkn_ready"], q.due("qkn_ready"))
            q.e.wait_ge(sems["decay_ready"], q.due("decay_ready"))
            for t in range(NT):
                for h in range(H):
                    c = slice(P * t, P * t + P)
                    k = cv[:, H + h, c]
                    mm(psum[:, t, P * h:P * h + P], k, k, start=True, stop=True)
                    mm(psum[:, 2 + t, P * h:P * h + P], k, cv[:, h, c], start=True, stop=True)
                    nc.tensor.transpose(psum[:, 4 + t, P * h:P * h + P], k, ident)
                    ins = nc.tensor.transpose(psum[:, 6 + t, P * h:P * h + P], cv[:, 2 * H + h, c], ident)
            ins.then_inc(sems["qk_ready"], 1)

        def dve_mats(q):
            q.e.wait_ge(sems["qk_ready"], q.due("qk_ready"))
            V.tensor_tensor(decT, banks(2, 2, TH, P), decT, ALU.mult)
            for t in range(NT):
                for h in range(H):
                    j = t * H + h
                    ins = V.scalar_tensor_tensor(out=th(decN, t, h), in0=psum[:, t, P * h:P * h + P], scalar=beta[:, j:j + 1],
                                                 in1=th(decN, t, h), op0=ALU.mult, op1=ALU.mult)
            ins.then_inc(sems["mats_ready"], 1)
            V.tensor_tensor(cv[:, 0:H, :], cv[:, 0:H, :], egrow, ALU.mult)
            for t in range(NT):
                for h in range(H):
                    j = t * H + h
                    ins = V.tensor_scalar(kv[:, j, P:2 * P], psum[:, 6 + t, P * h:P * h + P], beta[:, j:j + 1], None, ALU.mult)
            ins.then_inc(sems["kv_ready"], 1)

        def dve_keys(q):
            q.e.wait_ge(sems["kv_read"], q.due("kv_read"))
            for t in range(NT):
                for h in range(H):
                    j = t * H + h
                    ins = V.tensor_scalar(kv[:, j, 0:P], psum[:, 4 + t, P * h:P * h + P], bg[:, j:j + 1], None, ALU.mult)
            ins.then_inc(sems["kv_ready"], 1)

        def act_mats(q):
            q.e.wait_ge(sems["qk_ready"], q.due("qk_ready"))
            q.e.wait_ge(sems["scales_ready"], q.due("scales_ready"))
            for t in range(NT):
                for h in range(H):
                    j = t * H + h
                    for par, dl in enumerate((dl0, dl1)):
                        ins = A.activation(kd[:, par, j, :], psum[:, 4 + t, P * h:P * h + P], ACT.Copy, scale=dl[:, j:j + 1])
            ins.then_inc(sems["kv_read"], 1)

        def each(fn, b0):
            for j in range(TH):
                lhs, rhs = fn(j)
                ins = mm(psum[:, b0 + j // H, P * (j % H):P * (j % H) + P], lhs, rhs, start=True, stop=True)
            return ins

        def pe_inverse(q):
            q.e.wait_ge(sems["mats_ready"], q.due("mats_ready"))
            for j in range(TH):
                ins = nc.tensor.transpose(psum[:, j // H, P * (j % H):P * (j % H) + P], decN[:, j, :], ident)
            ins.then_inc(sems["tri_ready"], 1)
            q.e.wait_ge(sems["kv_ready"], q.due("kv_ready"))
            pe_ada(q, 1, 6)
            q.e.wait_ge(sems["tri_read"], q.due("tri_read"))
            each(lambda j: (Lt[:, j, :], decN[:, j, :]), 0)
            each(lambda j: (decN[:, j, :], Lt[:, j, :]), 2).then_inc(sems["tri_ready"], 1)
            pe_ada(q, 1, 6)
            q.e.wait_ge(sems["kv_ready"], q.due("kv_ready"))
            q.e.wait_ge(sems["tri_read"], q.due("tri_read"))
            each(lambda j: (Lt2[:, j, :], L2[:, j, :]), 0)
            each(lambda j: (L2[:, j, :], Lt2[:, j, :]), 2)
            each(lambda j: (L2[:, j, :], Pt[:, j, :]), 4).then_inc(sems["tri_ready"], 1)
            pe_ada(q, 1, 6)
            q.e.wait_ge(sems["tri_read"], q.due("tri_read"))
            each(lambda j: (Lt4[:, j, :], L4[:, j, :]), 0)
            each(lambda j: (L4[:, j, :], Pt[:, j, :]), 4).then_inc(sems["tri_ready"], 1)
            pe_ada(q, 1, 6)
            q.e.wait_ge(sems["tri_read"], q.due("tri_read"))
            each(lambda j: (L8[:, j, :], Pt[:, j, :]), 4).then_inc(sems["tri_ready"], 1)
            pe_ada(q, 1, 6)
            pe_ada_end(q)
            q.e.wait_ge(sems["tri_read"], q.due("tri_read"))
            each(lambda j: (Em[:, j, :], Pt[:, j, :]), 0)
            each(lambda j: (Pt[:, j, :], Em[:, j, :]), 2)
            for j in range(TH):
                ins = mm(psum[:, 4 + j // 2, 256 * (j % 2):256 * (j % 2) + 256], Pt[:, j, :], kv[:, j, :], start=True, stop=True)
            ins.then_inc(sems["tri_ready"], 1)
            q.e.wait_ge(sems["tri_read"], q.due("tri_read"))
            each(lambda j: (Fm[:, j, :], Ft[:, j, :]), 0)
            for j in range(TH):
                ins = mm(psum[:, 4 + j // 2, 256 * (j % 2):256 * (j % 2) + 256], Ft[:, j, :], kv[:, j, :], start=True, stop=True)
            ins.then_inc(sems["tri_ready"], 1)
            pe_ada(q, 1, 2)
            q.e.wait_ge(sems["tri_read"], q.due("tri_read"))
            for j in range(TH):
                ins = mm(psum[:, 4 + j // 2, 256 * (j % 2):256 * (j % 2) + 256], Ft2[:, j, :], kv[:, j, :], start=True, stop=True)
            ins.then_inc(sems["tri_ready"], 1)
            pe_ada(q, 1, 2)
            q.e.wait_ge(sems["tri_read"], q.due("tri_read"))
            for j in range(TH):
                ins = nc.tensor.transpose(psum[:, j // H, P * (j % H):P * (j % H) + P], kv[:, j, 0:P], ident)
            ins.then_inc(sems["tri_ready"], 1)
            pe_ada(q, 1, 2)
            q.e.wait_ge(sems["tri_read"], q.due("tri_read"))

        def dve_inverse(q):
            b02, b22, b42 = (banks(b, 2, TH, P) for b in (0, 2, 4))
            wide = banks(4, 4, TH, 2 * P)
            q.e.wait_ge(sems["tri_ready"], q.due("tri_ready"))
            blk, off = over(v("blk16"), TH), over(v("off16"), TH)
            V.tensor_tensor(Em, decN, off, ALU.mult)
            V.tensor_tensor(Lt, b02, blk, ALU.mult).then_inc(sems["dve_step"], 1)
            q.e.wait_ge(sems["dve_step"], q.due("dve_step"))
            V.tensor_tensor(decN, decN, blk, ALU.mult)
            V.tensor_tensor(Pt, over(ident, TH), Lt, ALU.subtract).then_inc(sems["tri_read"], 1)
            dve_keys(q)
            q.e.wait_ge(sems["tri_ready"], q.due("tri_ready"))
            V.tensor_copy(L2, b02)
            V.tensor_copy(Lt2, b22).then_inc(sems["tri_read"], 1)
            q.e.wait_ge(sems["tri_ready"], q.due("tri_ready"))
            V.tensor_copy(L4, b02)
            V.tensor_copy(Lt4, b22)
            V.tensor_tensor(Pt, b42, Pt, ALU.add).then_inc(sems["tri_read"], 1)
            q.e.wait_ge(sems["tri_ready"], q.due("tri_ready"))
            V.tensor_copy(L8, b02)
            V.tensor_tensor(Pt, b42, Pt, ALU.add).then_inc(sems["tri_read"], 1)
            q.e.wait_ge(sems["tri_ready"], q.due("tri_ready"))
            V.tensor_tensor(Pt, b42, Pt, ALU.add).then_inc(sems["tri_read"], 1)
            q.e.wait_ge(sems["tri_ready"], q.due("tri_ready"))
            V.tensor_copy(Ft, b02)
            V.tensor_copy(Fm, b22)
            V.tensor_copy(kv, wide).then_inc(sems["tri_read"], 1)
            q.e.wait_ge(sems["tri_ready"], q.due("tri_ready"))
            V.tensor_copy(Ft2, b02)
            V.tensor_tensor(kv, kv, wide, ALU.subtract).then_inc(sems["tri_read"], 1)
            q.e.wait_ge(sems["tri_ready"], q.due("tri_ready"))
            V.tensor_tensor(kv, kv, wide, ALU.add).then_inc(sems["tri_read"], 1)
            q.e.wait_ge(sems["tri_ready"], q.due("tri_ready"))
            V.tensor_copy(wT, b02).then_inc(sems["tri_read"], 1)

        def pe_delta_scan(q):
            q.e.wait_ge(sems["state_ready"], q.due("state_ready"))
            for c in range(NCH):
                t, par = c // 2, c % 2
                for h in range(H):
                    ins = mm(psum[:, 0, P * h:P * h + P], wT[:, t * H + h, :], Sst[:, h, :], start=True, stop=True)
                ins.then_inc(sems["wstate_ready"], 1)
                pe_ada(q, 1, 2)
                q.e.wait_ge(sems["vnew_ready"], q.due("vnew_ready"))
                for h in range(H):
                    ins = mm(psum[:, 1, P * h:P * h + P], kd[:, par, t * H + h, :], vnew[:, h, :], start=True, stop=True)
                ins.then_inc(sems["dstate_ready"], 1)
                for h in range(H):
                    o = banks(4, 2, H, S)[:, h, CH * c:CH * c + CH]
                    mm(o, Sst[:, h, :], cv[:, h, CH * c:CH * c + CH], start=True, stop=False, skip_group_check=True)
                    ins = mm(o, vnew[:, h, :], decT[:, t * H + h, CH * par:CH * par + CH], start=False, stop=True,
                             skip_group_check=True)
                ins.then_inc(sems["scan_out"], 1)
                if c < NCH - 1:
                    q.e.wait_ge(sems["state_ready"], q.due("state_ready"))
            pe_ada_end(q)

        def act_delta_ada(q):
            act_ada(q, ADA_STEPS[2], 6)
            act_ada_end(q)
            act_ada(q, ADA_STEPS[3] + ADA_STEPS[4], 2)
            act_ada_end(q)

        def dve_delta_scan(q):
            V.memset(vnew, 0.0)
            V.memset(Sst, 0.0).then_inc(sems["state_ready"], 1)
            q.e.wait_ge(sems["state_ready"], q.due("state_ready"))
            for c in range(NCH):
                t, par = c // 2, c % 2
                r = slice(CH * par, CH * par + CH)
                q.e.wait_ge(sems["wstate_ready"], q.due("wstate_ready"))
                V.tensor_tensor(vnew[r], kv[r, t * H:t * H + H, P:2 * P],
                                psum[r, 0, :].rearrange("p (a b) -> p a b", a=H), ALU.subtract).then_inc(sems["vnew_ready"], 1)
                if c < NCH - 1:
                    q.e.wait_ge(sems["dstate_ready"], q.due("dstate_ready"))
                    q.e.wait_ge(sems["scan_out"], q.due("scan_out"))
                    for h in range(H):
                        ins = V.scalar_tensor_tensor(
                            out=Sst[:, h, :], in0=Sst[:, h, :], scalar=egrow[:, h, CH * c + CH - 1:CH * c + CH],
                            in1=psum[:, 1, P * h:P * h + P], op0=ALU.mult, op1=ALU.add)
                    ins.then_inc(sems["state_ready"], 1)
            q.skip("dstate_ready")
            q.skip("scan_out")
            q.skip("state_ready", NCH - 1)

        def act_delta_out(q):
            q.e.wait_ge(sems["scan_out"], q.due("scan_out", NCH))
            A.activation(osq[:, 0:H, :], banks(4, 2, H, S), ACT.Square, scale=P ** -0.5).then_inc(sems["sq_ready"], 1)
            act_root_table(q)
            act_root(q, osq[:, H:, :], banks(2, 2, H, S))

        def pe_delta_out(q):
            q.e.wait_ge(sems["sq_ready"], q.due("sq_ready"))
            for j in range(2):
                ins = mm(psum[:, 2 + j, :], ones, osq[:, 2 * j:2 * j + 2, :].rearrange("p a b -> p (a b)"), start=True, stop=True)
            ins.then_inc(sems["moment_ready"], 1)

        def dve_delta_out(q):
            q.e.wait_ge(sems["root_ready"], q.due("root_ready"))
            q.skip("moment_ready")
            V.reciprocal(osq[:, H:, :], osq[:, H:, :]).then_inc(sems["dve_step"], 1)
            q.e.wait_ge(sems["dve_step"], q.due("dve_step"))
            V.tensor_tensor(mix[:, 0:H, :], banks(4, 2, H, S), osq[:, H:, :], ALU.mult).then_inc(sems["dve_step"], 1)
            q.e.wait_ge(sems["dve_step"], q.due("dve_step"))
            V.scalar_tensor_tensor(out=mix[:, 0:H, :], in0=mix[:, 0:H, :], scalar=v("gdn_norm"), in1=zs,
                                   op0=ALU.mult, op1=ALU.mult).then_inc(sems["mix_ready"], 1)

        EVEN_OUT = (7, 6, 0, 1)

        def pe_even(q):
            pe_even_in(q)
            pe_rope(q)
            pe_sparse(q)
            q.e.wait_ge(sems["attn_read"], q.due("attn_read"))
            pe_qk(q)
            pe_inverse(q)
            pe_delta_scan(q)
            pe_delta_out(q)
            pe_out(q, mix, range(H, KD), range(H), EVEN_OUT)

        def act_even(q):
            q.e.wait_ge(sems["constants_in"], q.due("constants_in", 16))
            act_even_in(q)
            act_sparse(q)
            act_mats(q)
            act_delta_ada(q)
            act_delta_out(q)
            q.skip("unit_done", 4)

        def dve_even(q):
            q.e.wait_ge(sems["constants_in"], q.due("constants_in", 16))
            q.skip("unit_done", 17 + sum(ADA_STEPS))
            dve_gates(q)
            dve_conv(q)
            dve_decay(q)
            dve_qk(q)
            dve_rope(q)
            dve_sparse(q)
            dve_scales(q)
            q.e.wait_ge(sems["attn_read"], q.due("attn_read"))
            dve_mats(q)
            dve_inverse(q)
            dve_delta_scan(q)
            dve_delta_out(q)
            dve_ada(q, 0, ADA - ADA_FIRST, 16, 48)
            dve_residual(q, 16, EVEN_OUT)

        gq, gk = view(A0, H, S), view(A0 + 1024, H, S)
        gv = view(A0 + 2048, NT, D)
        gr = view(A0 + 4096, KD, S)
        gmix = view(A0 + 6144, KD, S)
        glr = view(A0 + 8192, S)
        la = view(A0 + 8448, H, S)
        eq, ek, eb, ed = (view(A0 + 9472 + 1024 * j, H, S) for j in range(4))
        att = view(A0 + 13568, 2, TH, CH)
        gkd = view(A0 + 14592, 2, TH, P)
        gS = view(A0 + 16640, H, S)
        ebl = view(A0 + 17664, H * NCH)
        gsq = view(A0, KD, S)

        def pe_gla_in(q):
            u = Units(q)
            s = slot(q)
            for k in range(KD):
                q.e.wait_ge(sems["norm_ready"], q.due("norm_ready"))
                ins = mm(psum[0:16, 5, 0:S], sl(s, KD)[:, k, 0:16], hT[:, k, :], start=(k == 0), stop=(k == KD - 1))
            ins.then_inc(sems["unit_done"], 1)
            for j in range(2):
                s = slot(q)
                for n in range(2):
                    pe_features(u, s, hT, 2 * P * n)
                if j == 0:
                    q.e.wait_ge(sems["glr_ready"], q.due("glr_ready"))
                    for h in range(H):
                        ins = mm(banks(6, 2, H, S)[:, h, :], v("gla_w2")[0:16, P * h:P * h + P], glr[0:16, :], start=True, stop=True)
                    ins.then_inc(sems["cums_ready"], 1)
            for j in range(2):
                s = slot(q)
                for t in range(NT):
                    pe_tokens(u, s, hT, 0, 512, t)
            u.end()

        def act_gla_in(q):
            q.e.wait_ge(sems["unit_done"], q.due("unit_done"))
            A.activation(glr[0:16, :], psum[0:16, 5, 0:S], ACT.Copy).then_inc(sems["glr_ready"], 1)
            for j in range(2):
                act_unit(q, j, gq[:, 2 * j:2 * j + 2, :], shape=2, scale=P ** -0.5)
            act_gla_gates(q)
            for j in range(2):
                act_unit(q, 2 + j, gk[:, 2 * j:2 * j + 2, :], shape=2)
            for n in range(4):
                act_unit(q, n, gv[:, n % 2, 512 * (n // 2):512 * (n // 2) + 512])
                if n == 0:
                    act_gla_gates2(q)

        def pe_gla_fill(q, n):
            c, j = n // 2, n % 2
            if n % 4 == 0:
                q.gate_slot = slot(q)
            if j == 0 and c >= 2:
                q.e.wait_ge(sems["fill_read"], q.due("fill_read"))
            ins = accumulate(psum[:, c % 2, S * j:S * j + S],
                             [(sl(q.gate_slot, KD)[:, k, P * (n % 4):P * (n % 4) + P], hT[:, k, :]) for k in range(KD)])
            if j == 1:
                ins.then_inc(sems["unit_done"], 1)

        def act_gla_fill(q, c):
            q.e.wait_ge(sems["unit_done"], q.due("unit_done"))
            A.activation(gr[:, 2 * c:2 * c + 2, :], banks(c % 2, 1, 2, S), ACT.Silu).then_inc(sems["fill_read"], 1)

        def dve_gla_gates(q):
            q.e.wait_ge(sems["cums_ready"], q.due("cums_ready"))
            b2 = v("gla_b2")
            for h in range(H):
                ins = V.tensor_scalar(la[:, h, :], banks(6, 2, H, S)[:, h, :], b2[:, h:h + 1], None, ALU.add)
            ins.then_inc(sems["dve_step"], 1)
            q.e.wait_ge(sems["dve_step"], q.due("dve_step"))
            V.scalar_tensor_tensor(out=eq, in0=la, scalar=-1.0, in1=la, op0=ALU.mult, op1=ALU.max).then_inc(sems["gexp_pre"], 1)
            q.e.wait_ge(sems["gexp_ready"], q.due("gexp_ready"))
            V.scalar_tensor_tensor(out=ek, in0=la, scalar=0.0, in1=eq, op0=ALU.min, op1=ALU.subtract).then_inc(sems["dve_step"], 1)
            q.e.wait_ge(sems["dve_step"], q.due("dve_step"))
            for h in range(H):
                ins = V.tensor_tensor_scan(la[:, h, :], v("run"), ek[:, h, :], 0.0, ALU.mult, ALU.add)
            ins.then_inc(sems["dve_step"], 1)
            q.e.wait_ge(sems["dve_step"], q.due("dve_step"))
            c = la.rearrange("p h (c i) -> p (h c) i", i=CH)
            mid, last = c[:, :, CH // 2 - 1], c[:, :, CH - 1]
            cut = 80.0 * TAU
            V.tensor_tensor(eq.rearrange("p h (c i) -> p (h c) i", i=CH), c, along(mid, CH), ALU.subtract).then_inc(sems["dve_step"], 1)
            q.e.wait_ge(sems["dve_step"], q.due("dve_step"))
            V.tensor_tensor(ed.rearrange("p h (c i) -> p (h c) i", i=CH), c, along(last, CH), ALU.subtract)
            V.tensor_scalar(eq, eq, cut, -cut, ALU.min, ALU.max).then_inc(sems["dve_step"], 1)
            q.e.wait_ge(sems["dve_step"], q.due("dve_step"))
            V.tensor_copy(ebl, last).then_inc(sems["gscan_ready"], 1)

        def act_gla_gates(q):
            q.e.wait_ge(sems["gexp_pre"], q.due("gexp_pre"))
            A.activation(eq, eq, ACT.Exp, scale=-1.0).then_inc(sems["act_step"], 1)
            q.e.wait_ge(sems["act_step"], q.due("act_step"))
            A.activation(eq, eq, ACT.Ln, bias=ONE).then_inc(sems["gexp_ready"], 1)

        def act_gla_gates2(q):
            q.e.wait_ge(sems["gscan_ready"], q.due("gscan_ready"))
            A.activation(ek, eq, ACT.Exp, scale=-1.0 / TAU)
            A.activation(eb, la, ACT.Exp, scale=1.0 / TAU)
            A.activation(ed, ed, ACT.Exp, scale=-1.0 / TAU)
            A.activation(ebl, ebl, ACT.Exp, scale=1.0 / TAU).then_inc(sems["act_step"], 1)
            q.e.wait_ge(sems["act_step"], q.due("act_step"))
            A.activation(eq, eq, ACT.Exp, scale=1.0 / TAU).then_inc(sems["gexp_ready"], 1)

        def dve_gla_qk(q):
            q.e.wait_ge(sems["gexp_ready"], q.due("gexp_ready"))
            q.e.wait_ge(sems["lin_read"], q.due("lin_read", 4))
            V.tensor_tensor(eq, gq, eq, ALU.mult)
            V.tensor_tensor(ek, gk, ek, ALU.mult)
            V.tensor_tensor(eb, gq, eb, ALU.mult)
            V.tensor_tensor(ed, gk, ed, ALU.mult).then_inc(sems["gq_ready"], 1)

        def pe_gla_att(q):
            q.e.wait_ge(sems["gq_ready"], q.due("gq_ready"))
            for t in range(NT):
                for h in range(H):
                    for par in range(2):
                        c = slice(P * t + CH * par, P * t + CH * par + CH)
                        j = t * H + h
                        mm(psum[CH * par:CH * par + CH, 0, CH * j:CH * j + CH], ek[:, h, c], eq[:, h, c], start=True, stop=True)
            for t in range(NT):
                for h in range(H):
                    ins = nc.tensor.transpose(psum[:, 1 + t, P * h:P * h + P], ed[:, h, P * t:P * t + P], ident)
            ins.then_inc(sems["att_ready"], 1)

        def dve_gla_att(q):
            q.e.wait_ge(sems["att_ready"], q.due("att_ready"))
            half = v("half", 2, CH)
            for par in range(2):
                V.tensor_tensor(att[:, par], banks(0, 1, TH, CH), over(half[:, par, :], TH), ALU.mult)
                V.tensor_scalar(gkd[:, par], banks(1, 2, TH, P), v("par")[:, par:par + 1], None, ALU.mult)
            V.memset(gS, 0.0).then_inc(sems["att_read"], 1)
            q.e.wait_ge(sems["att_read"], q.due("att_read"))

        def pe_gla_scan(q):
            q.e.wait_ge(sems["att_read"], q.due("att_read"))
            outs = banks(4, 4, 2 * H, S)
            for c in range(NCH):
                t, par = c // 2, c % 2
                if c > 0:
                    q.e.wait_ge(sems["state_ready"], q.due("state_ready"))
                for h in range(H):
                    ins = mm(psum[:, 2 + h // 2, S * (h % 2):S * (h % 2) + S], gkd[:, par, t * H + h, :], gv[:, t, S * h:S * h + S],
                             start=True, stop=True)
                ins.then_inc(sems["dstate_ready"], 1)
                for h in range(H):
                    for i in range(2):
                        o = outs[:, 2 * h + i, CH * c:CH * c + CH]
                        mm(o, gS[:, h, P * i:P * i + P], eb[:, h, CH * c:CH * c + CH], start=True, stop=False, skip_group_check=True)
                        ins = mm(o, gv[:, t, S * h + P * i:S * h + P * i + P], att[:, par, t * H + h, :], start=False, stop=True,
                                 skip_group_check=True)
                ins.then_inc(sems["scan_out"], 1)
                pe_gla_fill(q, c)
            pe_gla_fill(q, NCH)

        def dve_gla_scan(q):
            for c in range(NCH - 1):
                q.e.wait_ge(sems["dstate_ready"], q.due("dstate_ready"))
                q.e.wait_ge(sems["scan_out"], q.due("scan_out"))
                for h in range(H):
                    ins = V.scalar_tensor_tensor(out=gS[:, h, :], in0=gS[:, h, :], scalar=ebl[:, NCH * h + c:NCH * h + c + 1],
                                                 in1=psum[:, 2 + h // 2, S * (h % 2):S * (h % 2) + S], op0=ALU.mult, op1=ALU.add)
                ins.then_inc(sems["state_ready"], 1)
            q.skip("dstate_ready")
            q.skip("scan_out")

        def act_gla_out(q):
            act_gla_fill(q, 0)
            q.e.wait_ge(sems["scan_out"], q.due("scan_out", NCH))
            A.activation(gsq, banks(4, 4, 2 * H, S), ACT.Square, scale=S ** -0.5).then_inc(sems["sq_ready"], 1)
            act_gla_fill(q, 1)
            act_root_table(q)
            act_root(q, eq, banks(2, 2, H, S))
            for h in range(2, H):
                act_gla_fill(q, h)
            q.skip("fill_read", H)

        def pe_gla_out(q):
            q.e.wait_ge(sems["sq_ready"], q.due("sq_ready"))
            for h in range(H):
                ins = accumulate(banks(2, 2, H, S)[:, h, :], [(ones, gsq[:, 2 * h + i, :]) for i in range(2)])
            ins.then_inc(sems["moment_ready"], 1)
            for n in range(NCH + 1, 2 * H):
                pe_gla_fill(q, n)

        def dve_gla_out(q):
            q.e.wait_ge(sems["root_ready"], q.due("root_ready"))
            q.skip("moment_ready")
            V.reciprocal(eq, eq).then_inc(sems["dve_step"], 1)
            q.e.wait_ge(sems["dve_step"], q.due("dve_step"))
            m = gmix.rearrange("p (h i) s -> p h i s", i=2)
            r = gr.rearrange("p (h i) s -> p h i s", i=2)
            o = banks(4, 4, 2 * H, S).rearrange("p (h i) s -> p h i s", i=2)
            V.tensor_tensor(m[:, :, 0, :], o[:, :, 0, :], eq, ALU.mult)
            V.tensor_tensor(m[:, :, 1, :], o[:, :, 1, :], eq, ALU.mult).then_inc(sems["dve_step"], 1)
            q.e.wait_ge(sems["dve_step"], q.due("dve_step"))
            for h in (0, 2):
                q.e.wait_ge(sems["fill_read"], q.due("fill_read", 2))
                for i in range(2):
                    x = m[:, h:h + 2, i, :]
                    ins = V.scalar_tensor_tensor(out=x, in0=x, scalar=v("gla_norm")[:, i:i + 1], in1=r[:, h:h + 2, i, :],
                                                 op0=ALU.mult, op1=ALU.mult)
                ins.then_inc(sems["mix_ready"], 1)

        GLA_OUT = (2, 3, 4, 5)

        def pe_gla(q):
            pe_gla_in(q)
            pe_gla_att(q)
            pe_gla_scan(q)
            pe_gla_out(q)
            q.e.wait_ge(sems["mix_ready"], q.due("mix_ready"))
            pe_out(q, gmix, range(H), range(H, KD), GLA_OUT)
            q.e.wait_ge(sems["fill_read"], q.due("fill_read", 2))

        def act_gla(q):
            act_gla_in(q)
            act_gla_out(q)
            q.skip("unit_done", 4)

        def dve_gla(q):
            q.skip("unit_done", 13)
            dve_gla_gates(q)
            dve_gla_qk(q)
            q.skip("lin_read", 4)
            dve_gla_att(q)
            dve_gla_scan(q)
            dve_gla_out(q)
            dve_residual(q, 16, GLA_OUT)

        place = view(A0, NT, E, CAP)
        xN = view(A0 + 4096, NT, D)
        xg = view(A0 + 6144, KD, P)
        sil = view(A0 + 7168, 512)
        hid = view(A0 + 7680, 512)
        hidT = view(A0 + 8192, 4, P)
        ysl = view(A0 + 8704, D)
        gated = view(A0 + 9728, NT, P)
        gatedT = view(A0 + 9984, S)
        lg = view(A0 + 10240, NT, NG + E)
        g8 = view(A0 + 10320, NT, 8)
        top = view(A0 + 10336, NT, 2, 8)
        idx = view(A0 + 10368, NT, 2, 8).bitcast(U32)
        idf = view(A0 + 10400, NT, 2, 8)
        rt = view(A0 + 10432, NT, 16)
        ohg = view(A0 + 10464, NT, NG)
        el = view(A0 + 10480, NT, E)
        gates = view(A0 + 10544, NT, E)
        gtmp = view(A0 + 10608, NT, E)
        chosen = view(A0 + 10672, NT, E)
        rank = view(A0 + 10736, NT, E)
        most = view(A0 + 10800, 1)
        flags = view(PER + 88, 4).bitcast(I32)
        over_w13 = view(A0 + 10816, 2, KD, P)
        over_w2 = view(A0 + 12864, D)
        over_col = view(A0 + 13888, NT)
        over_gate = view(A0 + 13896, S)
        over_sil, over_hid = view(A0 + 14152, S), view(A0 + 14408, S)
        over_gates = view(A0 + 14664, NT, E)

        def pe_route(q, src, rw):
            w = v(rw, KD, NG + E)
            for k in range(KD):
                q.e.wait_ge(sems["norm_ready"], q.due("norm_ready"))
                for t in range(NT):
                    ins = mm(psum[:, 7, 40 * t:40 * t + NG + E], src[:, k, P * t:P * t + P], w[:, k, :],
                             start=(k + t == 0), stop=(k == KD - 1), skip_group_check=True)
            ins.then_inc(sems["router_ready"], 1)
            for t in range(NT):
                for k in range(KD):
                    ins = nc.tensor.transpose(banks(0, 4, NT, D)[:, t, P * k:P * k + P], src[:, k, P * t:P * t + P], ident)
            ins.then_inc(sems["tokens_turned"], 1)
            q.e.wait_ge(sems["route_done"], q.due("route_done"))
            mm(psum[:, 7, 128:160], v("cum"), chosen[:, 0, :], start=True, stop=True)
            accumulate(psum[:, 7, 160:192], [(ones, chosen[:, 0, :]), (v("cum"), chosen[:, 1, :])])
            accumulate(psum[:, 7, 192:224], [(ones, chosen[:, t, :]) for t in range(NT)]).then_inc(sems["ranks_ready"], 1)

        def dve_route(q, m):
            q.e.wait_ge(sems["router_ready"], q.due("router_ready"))
            V.memset(g8, OFF)
            V.tensor_tensor(lg, psum[:, 7, 0:80].rearrange("p (t n) -> p t n", t=NT)[:, :, 0:NG + E],
                            over(v(("rb0", "rb1", "rb_20", "rb_21")[m]), NT), ALU.add).then_inc(sems["dve_step"], 1)
            q.e.wait_ge(sems["dve_step"], q.due("dve_step"))
            V.tensor_copy(g8[:, :, 0:NG], lg[:, :, 0:NG]).then_inc(sems["dve_step"], 1)
            q.e.wait_ge(sems["dve_step"], q.due("dve_step"))
            for t in range(NT):
                ins = V.max(top[:, t, 0, :], g8[:, t, :])
            ins.then_inc(sems["dve_step"], 1)
            q.e.wait_ge(sems["dve_step"], q.due("dve_step"))
            for t in range(NT):
                V.max_index(idx[:, t, 0, :], top[:, t, 0, :], g8[:, t, :])
            V.tensor_scalar(rt[:, :, 0:1], top[:, :, 0, 0:1], -1.0, None, ALU.mult).then_inc(sems["dve_step"], 1)
            q.e.wait_ge(sems["dve_step"], q.due("dve_step"))
            V.tensor_copy(idf[:, :, 0, :], idx[:, :, 0, :]).then_inc(sems["route_pre"], 1)
            q.e.wait_ge(sems["route_pre"], q.due("route_pre"))
            for t in range(NT):
                ins = V.tensor_scalar(ohg[:, t, :], v("iota")[:, 0:NG], idf[:, t, 0, 0:1], None, ALU.is_equal)
            ins.then_inc(sems["dve_step"], 1)
            q.e.wait_ge(sems["dve_step"], q.due("dve_step"))
            V.tensor_scalar(ohg, ohg, 1.0, -OFF, ALU.subtract, ALU.mult).then_inc(sems["dve_step"], 1)
            q.e.wait_ge(sems["dve_step"], q.due("dve_step"))
            for t in range(NT):
                ins = V.tensor_tensor(el[:, t, :].rearrange("p (g e) -> p g e", g=NG),
                                      lg[:, t, NG:].rearrange("p (g e) -> p g e", g=NG), along(ohg[:, t, :], EG), ALU.add)
            ins.then_inc(sems["dve_step"], 1)
            q.e.wait_ge(sems["dve_step"], q.due("dve_step"))
            for t in range(NT):
                ins = V.max(top[:, t, 1, :], el[:, t, :])
            ins.then_inc(sems["dve_step"], 1)
            q.e.wait_ge(sems["dve_step"], q.due("dve_step"))
            for t in range(NT):
                V.max_index(idx[:, t, 1, :], top[:, t, 1, :], el[:, t, :])
            V.tensor_tensor(rt[:, :, 1:2], top[:, :, 1, 1:2], top[:, :, 1, 0:1], ALU.subtract).then_inc(sems["dve_step"], 1)
            q.e.wait_ge(sems["dve_step"], q.due("dve_step"))
            V.tensor_copy(idf[:, :, 1, :], idx[:, :, 1, :]).then_inc(sems["route_pre"], 1)
            q.e.wait_ge(sems["route_pre"], q.due("route_pre"))
            for t in range(NT):
                V.tensor_scalar(gates[:, t, :], v("iota"), idf[:, t, 1, 0:1], None, ALU.is_equal)
                ins = V.tensor_scalar(gtmp[:, t, :], v("iota"), idf[:, t, 1, 1:2], None, ALU.is_equal)
            ins.then_inc(sems["dve_step"], 1)
            q.e.wait_ge(sems["dve_step"], q.due("dve_step"))
            V.tensor_tensor(chosen, gates, gtmp, ALU.add).then_inc(sems["route_done"], 1)
            q.e.wait_ge(sems["route_done"], q.due("route_done"))
            q.e.wait_ge(sems["route_exp"], q.due("route_exp", 2))
            V.tensor_scalar(rt[:, :, 4:5], rt[:, :, 3:4], 1.0, None, ALU.add).then_inc(sems["dve_step"], 1)
            q.e.wait_ge(sems["dve_step"], q.due("dve_step"))
            V.tensor_tensor(rt[:, :, 4:5], rt[:, :, 4:5], rt[:, :, 2:3], ALU.mult).then_inc(sems["dve_step"], 1)
            q.e.wait_ge(sems["dve_step"], q.due("dve_step"))
            V.reciprocal(rt[:, :, 5:6], rt[:, :, 4:5]).then_inc(sems["dve_step"], 1)
            q.e.wait_ge(sems["dve_step"], q.due("dve_step"))
            V.tensor_tensor(rt[:, :, 6:7], rt[:, :, 5:6], rt[:, :, 3:4], ALU.mult).then_inc(sems["dve_step"], 1)
            q.e.wait_ge(sems["dve_step"], q.due("dve_step"))
            for t in range(NT):
                ins = V.tensor_scalar(gtmp[:, t, :], gtmp[:, t, :], rt[:, t, 6:7], None, ALU.mult)
            ins.then_inc(sems["dve_step"], 1)
            q.e.wait_ge(sems["dve_step"], q.due("dve_step"))
            for t in range(NT):
                V.scalar_tensor_tensor(out=gates[:, t, :], in0=gates[:, t, :], scalar=rt[:, t, 5:6], in1=gtmp[:, t, :],
                                       op0=ALU.mult, op1=ALU.add)
            q.e.wait_ge(sems["ranks_ready"], q.due("ranks_ready"))
            V.tensor_tensor(rank, psum[:, 7, 128:192].rearrange("p (t e) -> p t e", t=NT), chosen, ALU.mult).then_inc(sems["dve_step"], 1)
            q.e.wait_ge(sems["dve_step"], q.due("dve_step"))
            V.tensor_reduce(most, psum[:, 7, 192:224], AX.X, ALU.max)
            for t in range(NT):
                ins = V.tensor_tensor(place[:, t, 0:4, :], along(rank[:, t, 0:4], CAP), over(v("slots"), 4), ALU.is_equal)
            ins.then_inc(sems["place_ready"], 1)
            q.e.wait_ge(sems["place_ready"], q.due("place_ready"))
            V.tensor_copy(flags[:, m:m + 1], most)
            for t in range(NT):
                ins = V.tensor_tensor(place[:, t, 4:, :], along(rank[:, t, 4:], CAP), over(v("slots"), E - 4), ALU.is_equal)
            ins.then_inc(sems["place_ready"], 1)
            q.e.wait_ge(sems["place_ready"], q.due("place_ready"))

        def act_route(q):
            q.e.wait_ge(sems["route_pre"], q.due("route_pre"))
            for t in range(NT):
                ins = A.activation(rt[:, t, 8:12], lg[:, t, 0:NG], ACT.Exp, bias=rt[:, t, 0:1], accum_out=rt[:, t, 2:3])
            ins.then_inc(sems["route_exp"], 1)
            q.e.wait_ge(sems["route_pre"], q.due("route_pre"))
            A.activation(rt[:, :, 3:4], rt[:, :, 1:2], ACT.Exp).then_inc(sems["route_exp"], 1)
            q.e.wait_ge(sems["tokens_turned"], q.due("tokens_turned"))
            A.activation(xN, banks(0, 4, NT, D), ACT.Copy).then_inc(sems["tokens_ready"], 1)

        y = banks(4, 4, KD, S)

        def pe_clear(which):
            for b in which:
                mm(psum[:, b, :], v("zeros"), v("causal"), start=True, stop=False, skip_group_check=True)

        def pe_gather(q, pair):
            for k in range(KD):
                ins = accumulate(banks(2, 2, KD, P)[:, k, :],
                                 [(xN[:, t, P * k:P * k + P], place[:, t, pair, :].rearrange("p a b -> p (a b)"))
                                  for t in range(NT)])
            ins.then_inc(sems["gathered"], 1)

        def pe_scatter(q):
            for c in range(KD):
                ins = mm(y[:, c, :], ysl[:, P * c:P * c + P], gatedT, start=False, stop=False, skip_group_check=True)
            return ins

        def pe_pair(q, kind, pair, first, last):
            if kind == 1:
                for n in range(2):
                    w = [slot(q), slot(q)]
                    if n == 1 and not first:
                        q.e.wait_ge(sems["gatedT_ready"], q.due("gatedT_ready"))
                    for k in range(KD):
                        for e in range(2):
                            ins = mm(psum[CAP * e:CAP * e + CAP, n, :], xg[:, k, CAP * e:CAP * e + CAP], sl(w[e], KD)[:, k, :],
                                     start=(k == 0), stop=(k == KD - 1), skip_group_check=True)
                    ins.then_inc(sems["unit_done"], 1)
            else:
                w = [slot(q, 2), slot(q, 2)]
                for k in range(KD):
                    for e in range(2):
                        ins = mm(psum[CAP * e:CAP * e + CAP, 0, :], xg[:, k, CAP * e:CAP * e + CAP], sl(w[e], KD)[:, k, :],
                                 start=(k == 0), stop=(k == KD - 1), skip_group_check=True)
                ins.then_inc(sems["unit_done"], 1)
                if not first:
                    q.e.wait_ge(sems["gatedT_ready"], q.due("gatedT_ready"))
            if not first:
                q.e.wait_ge(sems["results_ready"], q.due("results_ready", 2))
            if not last:
                pe_gather(q, pair)
            fc = 4 if kind == 1 else 2
            q.e.wait_ge(sems["hid_ready"], q.due("hid_ready"))
            for f in range(fc):
                ins = nc.tensor.transpose(psum[:, 0, P * f:P * f + P], hid[:, P * f:P * f + P], ident)
            ins.then_inc(sems["hid_turned"], 1)
            if not first:
                pe_scatter(q)
            q.e.wait_ge(sems["hidT_ready"], q.due("hidT_ready"))
            if not last:
                q.e.wait_ge(sems["xg_ready"], q.due("xg_ready", 2))
            down = [slot(q), slot(q)] if kind == 1 else [slot(q, 2)] * 2
            for half in range(2):
                for f in range(fc):
                    for e in range(2):
                        row = f if kind == 1 else 2 * e + f
                        ins = mm(psum[CAP * e:CAP * e + CAP, 2 + half, :], hidT[:, f, CAP * e:CAP * e + CAP],
                                 sl(down[e], 4)[:, row, 512 * half:512 * half + 512], start=(f == 0), stop=(f == fc - 1),
                                 skip_group_check=True)
            ins.then_inc(sems["unit_done"], 1)
            q.e.wait_ge(sems["gated_ready"], q.due("gated_ready"))
            for t in range(NT):
                ins = nc.tensor.transpose(psum[:, 1, P * t:P * t + P], gated[:, t, :], ident)
            ins.then_inc(sems["gated_turned"], 1)

        def act_gathered(q):
            q.e.wait_ge(sems["gathered"], q.due("gathered"))
            A.activation(xg[:, 0:4, :], banks(2, 1, 4, P), ACT.Copy).then_inc(sems["xg_ready"], 1)

        def dve_gathered(q):
            q.e.wait_ge(sems["gathered"], q.due("gathered"))
            V.tensor_copy(xg[:, 4:8, :], banks(3, 1, 4, P)).then_inc(sems["xg_ready"], 1)

        def act_pair(q, kind, last):
            f = 512 if kind == 1 else 256
            q.e.wait_ge(sems["unit_done"], q.due("unit_done"))
            A.activation(sil[:, 0:f], psum[:, 0, 0:f], ACT.Silu).then_inc(sems["silu_ready"], 1)
            if not last:
                act_gathered(q)
            q.e.wait_ge(sems["hid_turned"], q.due("hid_turned"))
            A.activation(hidT[:, 0:f // P, :], banks(0, 1, f // P, P), ACT.Copy).then_inc(sems["hidT_ready"], 1)
            q.e.wait_ge(sems["unit_done"], q.due("unit_done", 2 if kind == 1 else 1))
            A.activation(ysl[:, 0:512], psum[:, 2, :], ACT.Copy).then_inc(sems["results_ready"], 1)

        def dve_pair(q, kind, pair, last):
            f = 512 if kind == 1 else 256
            if kind == 1:
                q.e.wait_ge(sems["unit_done"], q.due("unit_done", 2))
            q.e.wait_ge(sems["silu_ready"], q.due("silu_ready"))
            up = psum[:, 1, :] if kind == 1 else psum[:, 0, f:2 * f]
            V.tensor_tensor(hid[:, 0:f], up, sil[:, 0:f], ALU.mult).then_inc(sems["hid_ready"], 1)
            for t in range(NT):
                ins = V.tensor_tensor(gated[:, t, :].rearrange("p (e c) -> p e c", e=2), place[:, t, pair, :],
                                      along(gates[:, t, pair], CAP), ALU.mult)
            ins.then_inc(sems["gated_ready"], 1)
            if not last:
                dve_gathered(q)
            q.e.wait_ge(sems["unit_done"], q.due("unit_done", 1 if kind == 1 else 2))
            V.tensor_copy(ysl[:, 512:], psum[:, 3, :]).then_inc(sems["results_ready"], 1)
            q.e.wait_ge(sems["gated_turned"], q.due("gated_turned"))
            V.tensor_copy(gatedT, psum[:, 1, 0:S]).then_inc(sems["gatedT_ready"], 1)

        def experts_of(i, g, pairs, ahead=0):
            first = 2 * (i * pairs + g + ahead)
            return slice(first, first + 2) if isinstance(first, int) else bass.ds(first, 2)

        PAIRS = {1: 1, 2: 2}

        def pe_experts(q, kind, passes):
            n = PAIRS[kind]
            per = {f"slot{(q.slot + j) % NR}": 16 * kind for j in range(NR)}
            per.update(gatedT_ready=n, results_ready=2 * n, hid_ready=n, hidT_ready=n, xg_ready=2 * n, gated_ready=n)
            for g in range(n):
                pe_pair(q, kind, experts_of(0, g, n, 1), g == 0, False)
            with nc.tensor.Fori(1, passes - 1) as i:
                q.enter(i, per, 1)
                for g in range(n):
                    pe_pair(q, kind, experts_of(i, g, n, 1), False, False)
                q.leave(passes - 2)
            for g in range(n):
                pe_pair(q, kind, experts_of(passes - 1, g, n, 1), False, g == n - 1)
            q.e.wait_ge(sems["gatedT_ready"], q.due("gatedT_ready"))
            q.e.wait_ge(sems["results_ready"], q.due("results_ready", 2))
            pe_scatter(q).then_inc(sems["sum_done"], 1)

        def act_experts(q, kind, passes):
            n = PAIRS[kind]
            act_gathered(q)
            with nc.scalar.Fori(0, passes - 1) as i:
                q.enter(i, dict(unit_done=UNITS[kind], gathered=n, hid_turned=n))
                for g in range(n):
                    act_pair(q, kind, False)
                q.leave(passes - 1)
            for g in range(n):
                act_pair(q, kind, g == n - 1)

        def dve_experts(q, kind, passes):
            n = PAIRS[kind]
            dve_gathered(q)
            with nc.vector.Fori(0, passes - 1) as i:
                q.enter(i, dict(unit_done=UNITS[kind], silu_ready=n, gathered=n, gated_turned=n))
                for g in range(n):
                    dve_pair(q, kind, experts_of(i, g, n), False)
                q.leave(passes - 1)
            for g in range(n):
                dve_pair(q, kind, experts_of(passes - 1, g, n), g == n - 1)

        def over_sem(m, n):
            return sems[f"over_{n}{m}"]

        def pe_over(pe, m, src, fc):
            with pe.If(pe.value_load(flags[0:1, m:m + 1]) > CAP):
                mm(psum[:, 0, 0:S], v("zeros"), src[:, 0, :], start=True, stop=True).then_inc(over_sem(m, "used"), 1)
                with pe.Fori(0, E) as e:
                    pe.wait_ge(over_sem(m, "column"), e + 1)
                    for t in range(NT):
                        ins = mm(psum[:, 1, P * t:P * t + P], over_col[:, t:t + 1].broadcast_to([P, P]), ident, start=True, stop=True)
                    ins.then_inc(over_sem(m, "row"), 1)
                    for f in range(fc):
                        pe.wait_ge(over_sem(m, "loaded"), e * (48 * fc) + 48 * (f + 1))
                        for j in range(2):
                            ins = accumulate(psum[:, 0, S * j:S * j + S],
                                             [(over_w13[:, j, k, :], src[:, k, :]) for k in range(KD)])
                        ins.then_inc(over_sem(m, "up"), 1)
                        pe.wait_ge(over_sem(m, "hid"), e * fc + (f + 1))
                        for c in range(KD):
                            ins = mm(y[:, c, :], over_w2[:, P * c:P * c + P], over_hid, start=False, stop=False, skip_group_check=True)
                        ins.then_inc(over_sem(m, "used"), 1)

        def act_over(act, m, fc):
            with act.If(act.value_load(flags[0:1, m:m + 1]) > CAP):
                with act.Fori(0, E * fc) as n:
                    act.wait_ge(over_sem(m, "up"), n + 1)
                    A.activation(over_sil, psum[:, 0, 0:S], ACT.Silu).then_inc(over_sem(m, "silu"), 1)

        def dve_over(dve, m, fc):
            with dve.If(dve.value_load(flags[0:1, m:m + 1]) > CAP):
                V.tensor_scalar(over_gates, rank, CAP + 0.5, None, ALU.is_gt).then_inc(over_sem(m, "step"), 1)
                dve.wait_ge(over_sem(m, "step"), 1)
                V.tensor_tensor(over_gates, over_gates, gates, ALU.mult).then_inc(over_sem(m, "step"), 1)
                dve.wait_ge(over_sem(m, "step"), 2)
                with dve.Fori(0, E) as e:
                    V.tensor_copy(over_col, over_gates[:, :, bass.ds(e, 1)].rearrange("p t e -> p (t e)"))\
                        .then_inc(over_sem(m, "column"), 1)
                    dve.wait_ge(over_sem(m, "row"), e + 1)
                    V.tensor_copy(over_gate, psum[:, 1, 0:S]).then_inc(over_sem(m, "step"), 1)
                    dve.wait_ge(over_sem(m, "step"), e * (1 + fc) + 3)
                    for f in range(fc):
                        dve.wait_ge(over_sem(m, "silu"), e * fc + (f + 1))
                        V.tensor_tensor(over_sil, over_sil, over_gate, ALU.mult).then_inc(over_sem(m, "step"), 1)
                        dve.wait_ge(over_sem(m, "step"), e * (1 + fc) + (4 + f))
                        V.tensor_tensor(over_hid, psum[:, 0, S:2 * S], over_sil, ALU.mult).then_inc(over_sem(m, "hid"), 1)
                dve.wait_ge(over_sem(m, "used"), E * fc + 1)

        def pool_over(pool, m, w1, w3, w2, fc):
            pool.wait_ge(sems["place_ready"], 2 * (m + 1))
            with pool.If(pool.value_load(flags[0:1, m:m + 1]) > CAP):
                with pool.Fori(0, E) as e:
                    for f in range(fc):
                        pool.wait_ge(over_sem(m, "used"), e * fc + (f + 1))
                        for j, w in enumerate((w1, w3)):
                            pool.dma_start(over_w13[:, j], w[e, :, P * f:P * f + P].rearrange("(k p) n -> p k n", p=P))\
                                .then_inc(over_sem(m, "loaded"), 16)
                        pool.dma_start(over_w2, w2[e, P * f:P * f + P, :]).then_inc(over_sem(m, "loaded"), 16)

        def pe_moe(q, m, src, kind):
            pe_clear((4, 5))
            pe_route(q, src, ("rw0", "rw1", "rw_20", "rw_21")[m])
            pe_clear((6,))
            q.e.wait_ge(sems["tokens_ready"], q.due("tokens_ready"))
            q.e.wait_ge(sems["place_ready"], q.due("place_ready"))
            pe_gather(q, slice(0, 2))
            pe_clear((7,))
            q.e.wait_ge(sems["place_ready"], q.due("place_ready"))
            q.e.wait_ge(sems["xg_ready"], q.due("xg_ready", 2))
            pe_experts(q, kind, PASSES[kind])
            pe_over(q.e, m, src, 4 if kind == 1 else 2)

        def act_moe(q, m, kind):
            act_route(q)
            act_experts(q, kind, PASSES[kind])
            q.e.wait_ge(sems["place_ready"], q.due("place_ready", 2))
            act_over(q.e, m, 4 if kind == 1 else 2)

        def dve_moe(q, m, kind):
            dve_route(q, m)
            dve_experts(q, kind, PASSES[kind])
            q.e.wait_ge(sems["sum_done"], q.due("sum_done"))
            dve_over(q.e, m, 4 if kind == 1 else 2)


        def dve_moe_add(q, kind):
            for k in range(KD):
                if kind == 1:
                    ins = V.scalar_tensor_tensor(out=xT[:, k, :], in0=y[:, k, :], scalar=modc[:, 40 + k:41 + k], in1=xT[:, k, :],
                                                 op0=ALU.mult, op1=ALU.add)
                else:
                    ins = V.scalar_tensor_tensor(out=xT[:, k, :], in0=xT[:, k, :], scalar=ALPHA, in1=y[:, k, :],
                                                 op0=ALU.mult, op1=ALU.add)
                if k % 2 == 1:
                    ins.then_inc(sems["x_ready"], 1)
            q.e.wait_ge(sems["x_ready"], q.due("x_ready", 4))

        cq, ckv = view(A0, 2, S), view(A0 + 512, S)
        qm, km = view(A0 + 768, H, S), view(A0 + 1792, H, S)
        vm = view(A0 + 2816, NT, S)
        sbq, sbk = view(A0 + 3328, 2, S), view(A0 + 3840, 2, S)
        vsf = view(A0 + 4352, NT, 512)
        fxq, fxk = view(A0 + 5376, 2, S), view(A0 + 5888, 2, S)
        ca, cg = view(A0 + 6400, 2, S), view(A0 + 6912, 2, S)
        cysq = view(A0 + 6400, 2, S)
        crow = view(A0 + 6400, H, S)
        PADC = CONV2 - 1
        hp = view(A0 + 7424, 2, S + PADC)
        lnt = view(A0 + 7424, S)
        cy = view(A0 + 8000, 2, S)
        lf = view(A0 + 8512, NT, H)
        lfa, lfb = view(A0 + 8520, NT, H), view(A0 + 8528, NT, H)
        stat = rstd
        MA0 = A0 + 8544
        mla = Attention(MA0, range(H), 96.0 ** -0.5)
        fox = Attention(MA0, (0, 2, 1, 3), CH ** -0.5)
        sz, sl_, sn = (view(MA0 + 1536 * j, H, 3 * P) for j in range(3))
        mla_sq = view(MA0, 3, S)
        mt = view(MA0, 2, H, S)
        prod = view(MA0, 2, 4, S)
        merged = view(MA0 + 2048, KD, S)
        ysq = view(MA0, KD, S)
        gts = view(MA0 + 4608, 4, 4, S)
        ys = hT

        def w2(n, l, *dims):
            return v(f"{n}{l}", *dims)

        def pe_mix2_in(q, l):
            u = Units(q)
            s = slot(q)
            for n in range(2):
                pe_features(u, s, xT, 2 * P * n, q if n == 0 else None)
            s = slot(q, 2)
            pe_features(u, s, xT, 0)
            b = u.bank()
            accumulate(psum[:, b, 0:S], [(sl(s, KD)[:, k, 256:384], xT[:, k, :]) for k in range(KD)])
            accumulate(psum[CH:96, b, S:2 * S], [(sl(s, KD)[:, k, 384:416], xT[:, k, :]) for k in range(KD)])\
                .then_inc(sems["unit_done"], 1)
            b = u.bank()
            for t in range(NT):
                ins = accumulate(psum[:, b, H * t:H * t + H],
                                 [(xT[:, k, P * t:P * t + P], sl(s, KD)[:, k, 416:420]) for k in range(KD)])
            ins.then_inc(sems["unit_done"], 1)
            s = slot(q)
            for n in range(2):
                pe_features(u, s, xT, 2 * P * n)
            q.e.wait_ge(sems["sq_ready"], q.due("sq_ready"))
            accumulate(psum[:, 7, 0:S], [(ones, mla_sq[:, k, :]) for k in range(2)])
            mm(psum[:, 7, S:2 * S], ones, mla_sq[:, 2, :], start=True, stop=True).then_inc(sems["sum_ready"], 1)
            s = slot(q, 2)
            for t in range(NT):
                pe_tokens(u, s, xT, 0, 512, t)
            s = slot(q, 2)
            q.e.wait_ge(sems["mla_norm"], q.due("mla_norm"))
            uq = ring[:, s, 0:768].rearrange("p (k n) -> p k n", k=2)
            ukv = ring[:, s, 768:1280].rearrange("p (h n) -> p h n", h=H)
            for j in range(2):
                b = u.bank()
                for i in range(2):
                    h = 2 * j + i
                    ins = accumulate(psum[0:96, b, S * i:S * i + S], [(uq[:, k, 96 * h:96 * h + 96], cq[:, k, :]) for k in range(2)])
                ins.then_inc(sems["unit_done"], 1)
            for j in range(2):
                b = u.bank()
                for i in range(2):
                    ins = mm(psum[0:CH, b, S * i:S * i + S], ukv[:, 2 * j + i, 0:CH], ckv, start=True, stop=True)
                ins.then_inc(sems["unit_done"], 1)
            b = u.bank()
            for t in range(NT):
                ins = mm(psum[:, b, S * t:S * t + S], ckv[:, P * t:P * t + P], ukv[:, :, CH:2 * CH], start=True, stop=True)
            ins.then_inc(sems["unit_done"], 1)
            s = slot(q)
            pe_features(u, s, xT, 0)
            u.need(13)
            pe_mla_rotate(q)
            pe_features(u, s, xT, 2 * P)
            u.end()

        def act_mix2_in(q):
            act_unit(q, 0, ca, shape=2)
            act_unit(q, 1, cg, ACT.Sigmoid, shape=2)
            q.e.wait_ge(sems["unit_done"], q.due("unit_done"))
            A.activation(mla_sq[:, 0:2, :], banks(2, 1, 2, S), ACT.Square)
            A.activation(cq, banks(2, 1, 2, S), ACT.Copy).then_inc(sems["lin_read"], 1)
            q.e.wait_ge(sems["unit_done"], q.due("unit_done"))
            A.activation(mla_sq[:, 2, :], psum[:, 3, 0:S], ACT.Square).then_inc(sems["sq_ready"], 1)
            A.activation(ckv, psum[:, 3, 0:S], ACT.Copy)
            A.activation(km[CH:96, :, :], psum[CH:96, 3, S:2 * S].unsqueeze(1).broadcast_to([32, H, S]), ACT.Copy)\
                .then_inc(sems["lin_read"], 1)
            act_unit(q, 4, lf, n=NT * H, shape=NT)
            act_unit(q, 5, sbq, shape=2)
            act_unit(q, 6, sbk, shape=2)
            q.e.wait_ge(sems["sum_ready"], q.due("sum_ready"))
            A.activation(stat[:, 0, :], psum[:, 7, 0:S], ACT.Ln, bias=EPS5, scale=1.0 / 256)
            A.activation(stat[:, 1, :], psum[:, 7, S:2 * S], ACT.Ln, bias=EPS5, scale=1.0 / 128).then_inc(sems["act_step"], 1)
            q.e.wait_ge(sems["act_step"], q.due("act_step"))
            A.activation(stat, stat, ACT.Exp, scale=-0.5, bias=ZERO).then_inc(sems["rstd_ready"], 1)
            n = 7
            for t in range(NT):
                act_unit(q, n, vsf[:, t, :])
                n += 1
            for j in range(2):
                q.e.wait_ge(sems["unit_done"], q.due("unit_done"))
                A.activation(qm[0:96, 2 * j:2 * j + 2, :], psum[0:96, n % 4, :].rearrange("p (a b) -> p a b", a=2), ACT.Copy)\
                    .then_inc(sems["lin_read"], 1)
                n += 1
            for j in range(2):
                q.e.wait_ge(sems["unit_done"], q.due("unit_done"))
                A.activation(km[0:CH, 2 * j:2 * j + 2, :], psum[0:CH, n % 4, :].rearrange("p (a b) -> p a b", a=2), ACT.Copy)\
                    .then_inc(sems["lin_read"], 1)
                n += 1
            act_unit(q, n, vm, shape=2)
            act_unit(q, n + 1, fxq, shape=2)
            act_unit(q, n + 2, fxk, shape=2)

        def pe_fill(q, n, bank):
            pe_fill_read(q)
            for i in range(n):
                dc, j = q.filled // 4, q.filled % 4
                if j == 0:
                    q.gate_slot = slot(q, 4)
                accumulate(psum[:, bank, S * i:S * i + S],
                           [(sl(q.gate_slot, KD)[:, k, P * j:P * j + P], xT[:, k, :]) for k in range(KD)])\
                    .then_inc(sems["unit_done"], 1)
                q.filled += 1
            q.unread += 1

        def pe_fill_read(q):
            q.e.wait_ge(sems["fill_read"], q.due("fill_read", q.unread))
            q.unread = 0

        def act_fill(q, l, n, bank):
            q.e.wait_ge(sems["unit_done"], q.due("unit_done", n))
            b = w2("b_gate_2", l)
            for i in range(n):
                dc, j = q.filled // 4, q.filled % 4
                ins = A.activation(gts[:, dc, j, :], psum[:, bank, S * i:S * i + S], ACT.Identity,
                                   bias=b[:, j * KD + dc:j * KD + dc + 1])
                q.filled += 1
            ins.then_inc(sems["fill_read"], 1)

        FILL = dict(mla_logits=[(2, 7)], mla_turn=[(1, 7)], mla_values=[(1, 7)], sb_pre=[(2, 7), (1, 6)], sb_rev=[(2, 3)],
                    fox_logits=[(2, 7)], fox_turn=[(1, 7)], fox_values=[(2, 7), (2, 6)])

        def pe_fills(q, where):
            for n, bank in FILL[where]:
                pe_fill(q, n, bank)

        def act_fills(q, l, where):
            for n, bank in FILL[where]:
                act_fill(q, l, n, bank)

        def dve_mla_norm(q, l):
            q.e.wait_ge(sems["rstd_ready"], q.due("rstd_ready"))
            g = w2("q_norm_2", l)
            for k in range(2):
                V.scalar_tensor_tensor(out=cq[:, k, :], in0=cq[:, k, :], scalar=g[:, k:k + 1], in1=stat[:, 0, :],
                                       op0=ALU.mult, op1=ALU.mult)
            V.scalar_tensor_tensor(out=ckv, in0=ckv, scalar=w2("kv_norm_2", l), in1=stat[:, 1, :],
                                   op0=ALU.mult, op1=ALU.mult).then_inc(sems["mla_norm"], 1)

        def dve_conv2(q, l):
            q.e.wait_ge(sems["lin_read"], q.due("lin_read", 2))
            V.memset(hp[:, :, 0:PADC], 0.0)
            V.tensor_tensor(hp[:, :, PADC:], ca, cg, ALU.mult).then_inc(sems["dve_step"], 1)
            q.e.wait_ge(sems["dve_step"], q.due("dve_step"))
            w, b = w2("conv2_", l, 2, CONV2), w2("conv_b_2", l)
            for j in range(CONV2):
                for c in range(2):
                    x = hp[:, c, j:j + S]
                    if j == 0:
                        ins = V.tensor_scalar(cy[:, c, :], x, w[:, c, 0:1], b[:, c:c + 1], ALU.mult, ALU.add)
                    else:
                        ins = V.scalar_tensor_tensor(out=cy[:, c, :], in0=x, scalar=w[:, c, j:j + 1], in1=cy[:, c, :],
                                                     op0=ALU.mult, op1=ALU.add)
                if j < CONV2 - 1:
                    ins.then_inc(sems["dve_step"], 1)
                    q.e.wait_ge(sems["dve_step"], q.due("dve_step"))
            ins.then_inc(sems["conv_done"], 1)

        def pe_sums(q, src, sq, n, bank):
            q.e.wait_ge(sems["sq_ready"], q.due("sq_ready"))
            accumulate(psum[:, bank, S:2 * S], [(ones, src[:, k, :]) for k in range(n)])
            accumulate(psum[:, bank, 0:S], [(ones, sq[:, k, :]) for k in range(n)]).then_inc(sems["moment_ready"], 1)

        def dve_variance(q, n, total, squares):
            q.e.wait_ge(sems["moment_ready"], q.due("moment_ready"))
            V.tensor_scalar(stat[:, 0, :], total, 1.0 / (n * P), None, ALU.mult).then_inc(sems["dve_step"], 1)
            q.e.wait_ge(sems["dve_step"], q.due("dve_step"))
            V.tensor_tensor(lnt, stat[:, 0, :], stat[:, 0, :], ALU.mult).then_inc(sems["dve_step"], 1)
            q.e.wait_ge(sems["dve_step"], q.due("dve_step"))
            V.tensor_tensor(stat[:, 1, :], squares, lnt, ALU.subtract).then_inc(sems["var_ready"], 1)

        def act_deviation(q):
            q.e.wait_ge(sems["var_ready"], q.due("var_ready"))
            A.activation(stat[:, 1, :], stat[:, 1, :], ACT.Sqrt, bias=EPS5).then_inc(sems["root_ready"], 1)

        def dve_centre(q, x, n):
            V.tensor_tensor(x, x, over(stat[:, 0, :], n), ALU.subtract).then_inc(sems["dve_step"], 1)
            q.e.wait_ge(sems["dve_step"], q.due("dve_step"))
            q.e.wait_ge(sems["root_ready"], q.due("root_ready"))
            V.reciprocal(stat[:, 1, :], stat[:, 1, :]).then_inc(sems["dve_step"], 1)
            q.e.wait_ge(sems["dve_step"], q.due("dve_step"))
            return V.tensor_tensor(x, x, over(stat[:, 1, :], n), ALU.mult)

        def dve_ln(q, g, bank):
            dve_variance(q, KD, psum[:, bank + 1, 0:S], psum[:, bank, 0:S])
            V.tensor_tensor(xT, xT, over(stat[:, 0, :], KD), ALU.subtract).then_inc(sems["dve_step"], 1)
            q.e.wait_ge(sems["dve_step"], q.due("dve_step"))
            q.e.wait_ge(sems["root_ready"], q.due("root_ready"))
            V.reciprocal(stat[:, 1, :], stat[:, 1, :]).then_inc(sems["dve_step"], 1)
            q.e.wait_ge(sems["dve_step"], q.due("dve_step"))
            for k in range(KD):
                V.scalar_tensor_tensor(out=xT[:, k, :], in0=xT[:, k, :], scalar=g[:, k:k + 1], in1=stat[:, 1, :],
                                       op0=ALU.mult, op1=ALU.mult).then_inc(sems["scaled_ready"], 1)

        def pe_mla_rotate(q):
            for n, x in enumerate((qm, km)):
                for j in range(2):
                    ins = mm(psum[0:96, 4 + 2 * n + j, :], v("rot_m")[0:96, 0:96],
                             x[0:96, 2 * j:2 * j + 2, :].rearrange("p a b -> p (a b)"), start=True, stop=True)
            ins.then_inc(sems["rot_ready"], 1)

        def pe_mla(q):
            q.e.wait_ge(sems["rope_ready"], q.due("rope_ready"))
            mla.pe_logits(q, lambda j, t: (qm[0:96, j, P * t:P * t + P], km[0:96, j, :]))
            pe_sums(q, cy, cysq, 2, 6)
            pe_fills(q, "mla_logits")
            mla.pe_turn(q)
            pe_fills(q, "mla_turn")
            mla.pe_values(q, lambda h, t: vm[:, t, CH * h:CH * h + CH], branch_out)
            pe_fills(q, "mla_values")

        def branch_out(h):
            return banks(0, 1, 2, S)[CH * (h % 2):CH * (h % 2) + CH, h // 2, :]

        def dve_rotate(q):
            q.e.wait_ge(sems["rot_ready"], q.due("rot_ready"))
            for n, x in enumerate((qm, km)):
                V.tensor_tensor(mt[0:96, n], banks(4 + 2 * n, 2, H, S)[0:96], over(sinM[0:96], H), ALU.mult)
                V.tensor_tensor(x[0:96], x[0:96], over(cosM[0:96], H), ALU.mult).then_inc(sems["dve_step"], 1)
                q.e.wait_ge(sems["dve_step"], q.due("dve_step"))
                ins = V.tensor_tensor(x[0:96], x[0:96], mt[0:96, n], ALU.add)
            ins.then_inc(sems["rope_ready"], 1)

        def dve_mla(q):
            for t in range(NT):
                mla.dve_max(q, t, over(v("causal", NT, S)[:, t, :], H))
            dve_variance(q, 2, psum[:, 6, S:2 * S], psum[:, 6, 0:S])
            for t in range(NT):
                mla.dve_probs(q, t)
            dve_centre(q, cy, 2).then_inc(sems["convg_ready"], 1)

        def act_attention(q, l, att, branch, name):
            for t in range(NT):
                att.act_exp(q, t)
            if branch == 0:
                act_deviation(q)
            act_fills(q, l, name + "_logits")
            att.act_turned(q)
            act_fills(q, l, name + "_turn")
            act_branch(q, branch)

        def act_branch(q, branch):
            q.e.wait_ge(sems["attn_ready"], q.due("attn_ready"))
            A.activation(ys[:, 2 * branch:2 * branch + 2, :], banks(0, 1, 2, S), ACT.Copy).then_inc(sems["attn_read"], 1)

        def pe_sb(q):
            q.e.wait_ge(sems["attn_read"], q.due("attn_read"))
            for h in range(H):
                half = slice(CH * (h % 2), CH * (h % 2) + CH)
                mm(psum[:, h, 0:S], sbk[half, h // 2, 0:P], sbq[half, h // 2, :], start=True, stop=True)
                ins = mm(psum[:, h, S:3 * P], sbk[half, h // 2, P:S], sbq[half, h // 2, P:S], start=True, stop=True)
            ins.then_inc(sems["sb_pre"], 1)
            pe_fills(q, "sb_pre")
            pe_fill_read(q)
            q.e.wait_ge(sems["sb_soft"], q.due("sb_soft"))
            for h in range(H):
                o = psum[:, 4 + h, :]
                mm(o[:, 0:S], v("ntail"), sn[:, h, 0:S], start=True, stop=False, skip_group_check=True)
                mm(o[:, P:S], v("nones"), sn[:, h, S:], start=False, stop=True, skip_group_check=True)
                ins = mm(o[:, S:3 * P], v("ntail"), sn[:, h, S:], start=True, stop=True, skip_group_check=True)
            ins.then_inc(sems["sb_rev"], 1)
            pe_fills(q, "sb_rev")
            q.e.wait_ge(sems["sb_prob"], q.due("sb_prob"))
            for h in range(H):
                o = branch_out(h)
                vh = lambda t: vsf[:, t, CH * h:CH * h + CH]
                mm(o, vh(0), sz[:, h, 0:S], start=True, stop=False, skip_group_check=True)
                ins = mm(o[:, P:S], vh(1), sz[:, h, S:], start=False, stop=True, skip_group_check=True)
            ins.then_inc(sems["attn_ready"], 1)

        def dve_sb(q):
            q.e.wait_ge(sems["sb_pre"], q.due("sb_pre"))
            z = banks(0, 4, H, 512)[:, :, 0:3 * P]
            V.scalar_tensor_tensor(out=sz, in0=z, scalar=CH ** -0.5, in1=over(v("strict"), H), op0=ALU.mult, op1=ALU.add).then_inc(sems["dve_step"], 1)
            q.e.wait_ge(sems["dve_step"], q.due("dve_step"))
            V.scalar_tensor_tensor(out=sl_, in0=sz, scalar=-1.0, in1=sz, op0=ALU.mult, op1=ALU.max).then_inc(sems["sb_abs"], 1)
            q.e.wait_ge(sems["sb_exp"], q.due("sb_exp"))
            V.scalar_tensor_tensor(out=sn, in0=sz, scalar=0.0, in1=sl_, op0=ALU.max, op1=ALU.add).then_inc(sems["sb_soft"], 1)
            q.e.wait_ge(sems["sb_rev"], q.due("sb_rev"))
            V.tensor_tensor(sz, sz, banks(4, 4, H, 512)[:, :, 0:3 * P], ALU.add).then_inc(sems["sb_arg"], 1)

        def act_sb(q, l):
            q.e.wait_ge(sems["sb_abs"], q.due("sb_abs"))
            A.activation(sl_, sl_, ACT.Exp, scale=-1.0).then_inc(sems["act_step"], 1)
            q.e.wait_ge(sems["act_step"], q.due("act_step"))
            A.activation(sl_, sl_, ACT.Ln, bias=ONE).then_inc(sems["sb_exp"], 1)
            act_fills(q, l, "sb_pre")
            q.e.wait_ge(sems["sb_arg"], q.due("sb_arg"))
            A.activation(sz, sz, ACT.Exp).then_inc(sems["sb_prob"], 1)
            act_fills(q, l, "sb_rev")
            act_branch(q, 1)

        def dve_forget(q, l):
            q.e.wait_ge(sems["lin_read"], q.due("lin_read", 3))
            V.tensor_tensor(lf, lf, over(w2("b_forget_2", l), NT), ALU.add).then_inc(sems["dve_step"], 1)
            q.e.wait_ge(sems["dve_step"], q.due("dve_step"))
            V.scalar_tensor_tensor(out=lfa, in0=lf, scalar=-1.0, in1=lf, op0=ALU.mult, op1=ALU.max).then_inc(sems["fox_pre"], 1)

        def dve_forget2(q):
            q.e.wait_ge(sems["fox_exp"], q.due("fox_exp"))
            V.scalar_tensor_tensor(out=lfb, in0=lf, scalar=0.0, in1=lfa, op0=ALU.min, op1=ALU.subtract).then_inc(sems["fox_gate"], 1)

        def act_forget(q):
            q.e.wait_ge(sems["fox_pre"], q.due("fox_pre"))
            A.activation(lfa, lfa, ACT.Exp, scale=-1.0).then_inc(sems["act_step"], 1)
            q.e.wait_ge(sems["act_step"], q.due("act_step"))
            A.activation(lfa, lfa, ACT.Ln, bias=ONE).then_inc(sems["fox_exp"], 1)

        def pe_fox(q):
            q.e.wait_ge(sems["fox_gate"], q.due("fox_gate"))
            for j, h in enumerate(fox.order):
                o = banks(4, 2, H, S)[:, j, :]
                g = [lfb[:, t, h:h + 1].broadcast_to([P, P]) for t in range(NT)]
                mm(o[:, 0:P], g[0], v("cum"), start=True, stop=True, skip_group_check=True)
                mm(o[:, P:S], g[0], ones, start=True, stop=False, skip_group_check=True)
                ins = mm(o[:, P:S], g[1], v("cum"), start=False, stop=True, skip_group_check=True)
            ins.then_inc(sems["fox_cum"], 1)
            pe_fill_read(q)
            q.e.wait_ge(sems["attn_read"], q.due("attn_read"))
            half = lambda h: slice(CH * (h % 2), CH * (h % 2) + CH)
            fox.pe_logits(q, lambda j, t: (fxq[half(fox.order[j]), fox.order[j] // 2, P * t:P * t + P],
                                           fxk[half(fox.order[j]), fox.order[j] // 2, :]))
            pe_fills(q, "fox_logits")
            q.e.wait_ge(sems["fox_row"], q.due("fox_row"))
            fox.pe_turn(q)
            pe_fills(q, "fox_turn")
            fox.pe_values(q, lambda h, t: vsf[:, t, S + CH * h:S + CH * h + CH], branch_out)
            pe_fills(q, "fox_values")
            pe_fill_read(q)
            q.e.wait_ge(sems["attn_read"], q.due("attn_read"))

        def dve_fox(q):
            q.e.wait_ge(sems["fox_cum"], q.due("fox_cum"))
            V.tensor_copy(crow, banks(4, 2, H, S)).then_inc(sems["fox_row"], 1)
            q.e.wait_ge(sems["fox_row"], q.due("fox_row"))
            for t in range(NT):
                q.e.wait_ge(sems["logits_ready"], q.due("logits_ready"))
                x = fox.lg[:, t]
                V.scalar_tensor_tensor(out=x, in0=banks(2 * t, 2, H, S), scalar=fox.scale, in1=crow,
                                       op0=ALU.mult, op1=ALU.subtract).then_inc(sems["dve_step"], 1)
                q.e.wait_ge(sems["dve_step"], q.due("dve_step"))
                V.tensor_tensor(x, x, over(v("causal", NT, S)[:, t, :], H), ALU.add).then_inc(sems["dve_step"], 1)
                q.e.wait_ge(sems["dve_step"], q.due("dve_step"))
                V.tensor_reduce(fox.nmax[:, t, :], x, AX.X, ALU.max, negate=True).then_inc(sems["max_ready"], 1)
            for t in range(NT):
                fox.dve_probs(q, t)

        def pe_merge(q):
            q.e.wait_ge(sems["branch_read"], q.due("branch_read"))
            late = [slot(q, 4), slot(q, 4)]
            br = [slot(q, 2), slot(q, 2)]
            for half in range(2):
                if half == 1:
                    u = Units(q)
                    q.e.wait_ge(sems["gts_read"], q.due("gts_read", 4))
                    for j in range(4):
                        s = late[j] if j < 2 else slot(q, 4)
                        for n in range(2):
                            pe_features(u, s, xT, 2 * P * n)
                    u.end()
                for j in range(4):
                    dc = 4 * half + j
                    if j >= 2:
                        q.e.wait_ge(sems["gate_read"], q.due("gate_read"))
                    for n in range(4):
                        ins = accumulate(banks(4 + 2 * (j % 2), 2, 4, S)[:, n, :],
                                         [(sl(br[n // 2], 4)[:, 2 * (n % 2) + k, P * dc:P * dc + P], ys[:, 2 * n + k, :])
                                          for k in range(2)])
                    ins.then_inc(sems["unit_done"], 1)
                q.skip("gate_read", 2)
            q.e.wait_ge(sems["gts_read"], q.due("gts_read", 2))
            pe_out(q, merged, range(KD - 2), range(KD - 2, KD), range(4))
            q.skip("gts_read")

        def act_merge(q, l):
            b = w2("b_gate_2", l)
            q.e.wait_ge(sems["fill_read"], q.due("fill_read", sum(len(f) for f in FILL.values())))
            for j in range(4):
                A.activation(gts[:, j], gts[:, j], ACT.Sigmoid).then_inc(sems["gts_ready"], 1)
            q.skip("unit_done", 4)
            for j in range(4):
                for n in range(4):
                    if n % 2 == 0:
                        q.e.wait_ge(sems["unit_done"], q.due("unit_done"))
                    if j == 0 and n == 0:
                        q.e.wait_ge(sems["gts_read"], q.due("gts_read", 4))
                    ins = A.activation(gts[:, j, n, :], psum[:, (2 * j + n // 2) % 4, S * (n % 2):S * (n % 2) + S], ACT.Sigmoid,
                                       bias=b[:, n * KD + 4 + j:n * KD + 5 + j])
                    if n % 2 == 1:
                        ins.then_inc(sems["lin_read"], 1)
            q.skip("gts_read", 3)
            q.skip("unit_done", 8)

        def dve_merge(q):
            q.skip("lin_read", 11)
            q.skip("unit_done", 16)
            for half in range(2):
                if half == 1:
                    q.skip("unit_done", 8)
                for j in range(4):
                    dc = 4 * half + j
                    q.e.wait_ge(sems["gts_ready" if half == 0 else "lin_read"], q.due("gts_ready" if half == 0 else "lin_read", 1 + half))
                    q.e.wait_ge(sems["unit_done"], q.due("unit_done"))
                    pr = prod[:, j % 2]
                    V.tensor_tensor(pr, banks(4 + 2 * (j % 2), 2, 4, S), gts[:, j], ALU.mult).then_inc(sems["gate_read"], 1)
                    q.e.wait_ge(sems["gate_read"], q.due("gate_read"))
                    ins = V.tensor_reduce(merged[:, dc, :], pr.rearrange("p n s -> p s n"), AX.X, ALU.add)
                    ins.then_inc(sems["gts_read" if dc < KD - 1 else "mix_ready"], 1)
            for b in range(4):
                q.e.wait_ge(sems["unit_done"], q.due("unit_done"))
                x = xT[:, 2 * b:2 * b + 2, :]
                V.scalar_tensor_tensor(out=x, in0=x, scalar=ALPHA, in1=psum[:, b, :].rearrange("p (a b) -> p a b", a=2),
                                       op0=ALU.mult, op1=ALU.add).then_inc(sems["x_ready"], 1)
            q.e.wait_ge(sems["x_ready"], q.due("x_ready", 4))

        def pe_mix2(q, l):
            q.filled = q.unread = 0
            pe_mix2_in(q, l)
            pe_mla(q)
            pe_sb(q)
            pe_fox(q)
            pe_merge(q)
            pe_square_sum(q, ysq, 6, True)

        def act_mix2(q, l):
            q.filled = 0
            act_mix2_in(q)
            act_forget(q)
            q.e.wait_ge(sems["conv_done"], q.due("conv_done"))
            A.activation(cysq, cy, ACT.Square, scale=(2 * P) ** -0.5).then_inc(sems["sq_ready"], 1)
            act_attention(q, l, mla, 0, "mla")
            act_fills(q, l, "mla_values")
            q.e.wait_ge(sems["convg_ready"], q.due("convg_ready"))
            g, b = w2("conv_ln_g_2", l), w2("conv_ln_b_2", l)
            for k in range(2):
                ins = A.activation(ys[:, 4 + k, :], cy[:, k, :], ACT.Silu, scale=g[:, k:k + 1], bias=b[:, k:k + 1])
            ins.then_inc(sems["branch_read"], 1)
            act_sb(q, l)
            act_attention(q, l, fox, 3, "fox")
            act_fills(q, l, "fox_values")
            act_merge(q, l)
            act_squares(q, ysq)
            act_deviation(q)
            act_shift(q, xT, w2("ln1_b_2", l))

        def dve_mix2(q, l):
            q.skip("unit_done", 16)
            dve_conv2(q, l)
            dve_mla_norm(q, l)
            dve_forget(q, l)
            dve_rotate(q)
            dve_mla(q)
            dve_forget2(q)
            dve_sb(q)
            dve_fox(q)
            dve_merge(q)
            dve_ln(q, w2("ln1_g_2", l), 6)

        @block.tensor
        def _(pe):
            q = Engine(pe)
            q.slot = q.ada = q.ada_read = 0
            q.ada_bank = None
            q.e.wait_ge(sems["inputs_in"], q.due("inputs_in", 64))
            for l in range(2):
                pe_square_sum(q, NSQ, 0 if l > 0 else 7)
                if l == 0:
                    q.e.wait_ge(sems["silu_c"], q.due("silu_c"))
                    pe_ada(q, ADA_FIRST, 0)
                    pe_ada_end(q)
                    pe_even(q)
                else:
                    pe_gla(q)
                pe_square_sum(q, NSQ, 7)
                pe_moe(q, l, hT, 1)
            pe_square_sum(q, NSQ, 0)
            for l in range(2):
                pe_mix2(q, l)
                pe_moe(q, 2 + l, xT, 2)
                pe_square_sum(q, ysq, 0, True)

        @block.scalar
        def _(act):
            q = Engine(act)
            q.ada, q.ada_bank = 0, None
            for j, n in enumerate(("positions", "positions_2")):
                act.dma_start(tab_pos[:, j, :], a[n].broadcast_to([P, S])).then_inc(sems["inputs_in"], 16)
            q.e.wait_ge(sems["inputs_in"], q.due("inputs_in", 64))
            A.activation(silc, v("c"), ACT.Silu).then_inc(sems["silu_c"], 1)
            act_squares(q, NSQ, False)
            act_root(q, rstd[:, 0, :], psum[:, 7, 0:S])
            act_tables(q)
            act_ada(q, ADA_FIRST, 0)
            act_ada_end(q)
            for l in range(2):
                if l > 0:
                    act_squares(q, NSQ)
                    act_root(q, rstd[:, 0, :], psum[:, 0, 0:S])
                act_shift(q, hT, modc[:, 0:8])
                if l == 0:
                    act_even(q)
                else:
                    act_gla(q)
                act_squares(q, NSQ)
                act_root(q, rstd[:, 0, :], psum[:, 7, 0:S])
                act_shift(q, hT, modc[:, 24:32])
                act_moe(q, l, 1)
            act_squares(q, NSQ)
            act_root(q, rstd[:, 0, :], psum[:, 0, 0:S])
            for l in range(2):
                act_mix2(q, l)
                act_moe(q, 2 + l, 2)
                act_squares(q, ysq)
                act_deviation(q)
                act_shift(q, xT, w2("ln2_b_2", l))

        @block.vector
        def _(dve):
            q = Engine(dve)
            q.e.wait_ge(sems["inputs_in"], q.due("inputs_in", 64))
            dve_tables(q)
            q.skip("unit_done", ADA_FIRST)
            for l in range(2):
                if l == 0:
                    dve_ada(q, 0, ADA_FIRST, 0, 16)
                else:
                    dve_ada(q, 1, ADA, 0, 48)
                dve_coef(q, 0, v(f"norm_mix{l}"))
                dve_norm(q, coef, hT, "scaled_ready")
                if l == 0:
                    q.e.wait_ge(sems["table_ready"], q.due("table_ready"))
                    V.memset(pre[:, :, 0:3], 0.0).then_inc(sems["dve_step"], 1)
                    q.e.wait_ge(sems["dve_step"], q.due("dve_step"))
                    dve_even(q)
                else:
                    dve_gla(q)
                dve_coef(q, 1, v(f"norm_ffn{l}"))
                dve_norm(q, coef, hT, "scaled_ready")
                dve_moe(q, l, 1)
                dve_moe_add(q, 1)
            dve_norm(q, v("final"), xT, "norm_ready")
            for l in range(2):
                dve_mix2(q, l)
                dve_moe(q, 2 + l, 2)
                dve_moe_add(q, 2)
                dve_ln(q, w2("ln2_g_2", l), 0)

        @block.gpsimd
        def _(pool):
            for l in range(2):
                pool_over(pool, l, a["exp_w1"][l], a["exp_w3"][l], a["exp_w2"][l], 4)
            for l in range(2):
                pool_over(pool, 2 + l, a["w_exp_gate_2"][l], a["w_exp_up_2"][l], a["w_exp_down_2"][l], 2)



BIG = ["ada_w", "even_w_in", "even_w_out", "gla_w_in", "gla_w_out", "exp_w1", "exp_w3", "exp_w2", "w_in_2", "mla_w_uq_2",
       "mla_w_ukv_2", "w_branch_2", "w_o_2", "w_exp_gate_2", "w_exp_up_2", "w_exp_down_2", "positions", "positions_2"]


def kernel(**inputs):
    import concourse.bacc as bacc
    from concourse.bass_utils import run_bass_kernel_spmd

    packed = {**constant_columns(), **parameter_columns(inputs)}
    packed = {n: packed[n] for n in EARLY + tuple(n for n in packed if n not in EARLY)}
    vec_at, at = {}, 0
    for name, c in packed.items():
        vec_at[name] = (at, c.shape[1])
        at += c.shape[1]
    arrays = {n: np.ascontiguousarray(inputs[n]) for n in BIG}
    arrays["xT"] = np.ascontiguousarray(np.asarray(inputs["x"])[0].T)
    arrays["vec"] = np.ascontiguousarray(np.concatenate(list(packed.values()), 1))

    nc = bacc.Bacc("TRN2", target_bir_lowering=False, num_devices=1)
    a = {n: nc.dram_tensor(f"in_{n}", x.shape, mybir.dt.from_np(x.dtype), kind="ExternalInput").ap()
         for n, x in arrays.items()}
    out = nc.dram_tensor("out", (D, S), F32, kind="ExternalOutput").ap()
    build(nc, a, vec_at, at, out)
    r = run_bass_kernel_spmd(nc, [{f"in_{n}": x for n, x in arrays.items()}], core_ids=[0])
    return np.ascontiguousarray(np.asarray(r.results[0]["out"]).T).reshape(1, S, D)
```
